# Optimizing a Trainium2 kernel written in Bass

```python
import math
import jax, jax.numpy as jnp
from jax import lax
import numpy as np

D_MODEL = 2048
BATCH = 1
SEQ = 512
DEPTH = 1
DEC_BATCH = 1
DEC_SEQ = 256
PAST_LEN = 128

ATTN_HEADS = 16
ATTN_HEAD_DIM = 128
ATTN_WIDTH = ATTN_HEADS * ATTN_HEAD_DIM
DILATED_PATTERNS = ((128, 1), (512, 4), (2048, 16))
N_BUCKETS = 32
BUCKET_MAX_DIST = 1024
SSM_HEADS = 32
SSM_HEAD_DIM = 64
SSM_WIDTH = SSM_HEADS * SSM_HEAD_DIM
SSM_GROUPS = 4
SSM_HEADS_PER_GROUP = SSM_HEADS // SSM_GROUPS
SSM_STATE = 128
CONV_WIDTH = 5
CHUNK = 128
CONV_CH = SSM_WIDTH + 2 * SSM_GROUPS * SSM_STATE
MIX_WIDTH = ATTN_WIDTH + SSM_WIDTH
IN_COLS = 4 * ATTN_WIDTH + SSM_WIDTH + CONV_CH + 2 * SSM_HEADS
EPS = 1e-6

kernel_name = "hybrid_dilated_attn_ssd_encoder"

def rmsnorm(x, g):
    xf = x.astype(jnp.float32)
    y = xf * lax.rsqrt(jnp.mean(xf * xf, axis=-1, keepdims=True) + EPS)
    return (y * g.astype(jnp.float32)).astype(x.dtype)

def t5_bucket(rel):
    nb = N_BUCKETS // 2
    max_exact = nb // 2
    ret = jnp.where(rel > 0, nb, 0)
    n = jnp.abs(rel)
    nf = jnp.maximum(n, 1).astype(jnp.float32)
    large = max_exact + (jnp.log(nf / max_exact) / math.log(BUCKET_MAX_DIST / max_exact)
                         * (nb - max_exact)).astype(jnp.int32)
    large = jnp.minimum(large, nb - 1)
    return ret + jnp.where(n < max_exact, n, large)

def banded_attention(q, k, v, bias, radius):
    bq, n, h, dh = q.shape
    nb = -(-n // radius)
    extra = nb * radius - n
    qb = jnp.pad(q, ((0, 0), (0, extra), (0, 0), (0, 0))).reshape(bq, nb, radius, h, dh)

    def neighbours(t):
        tb = jnp.pad(t, ((0, 0), (radius, extra + radius), (0, 0), (0, 0))).reshape(bq, nb + 2, radius, h, dh)
        return jnp.concatenate([tb[:, :-2], tb[:, 1:-1], tb[:, 2:]], axis=2)

    kb, vb = neighbours(k), neighbours(v)
    s = jnp.einsum("bnqhd,bnkhd->bnhqk", qb, kb, preferred_element_type=jnp.float32) * (1.0 / math.sqrt(dh))
    s = s + bias[None, None]
    qi = jnp.arange(radius)[:, None]
    kj = jnp.arange(3 * radius)[None, :]
    rel = kj - radius - qi
    key_pos = jnp.arange(nb)[:, None, None] * radius + kj[None] - radius
    valid = (jnp.abs(rel) <= radius)[None] & (key_pos >= 0) & (key_pos < n)
    s = jnp.where(valid[None, :, None], s, -jnp.inf)
    m = jnp.max(s, axis=-1, keepdims=True)
    p = jnp.exp(s - m)
    l = jnp.sum(p, axis=-1, keepdims=True)
    o = jnp.einsum("bnhqk,bnkhd->bnqhd", p, vb.astype(jnp.float32)) / jnp.swapaxes(l, 2, 3)
    lse = jnp.swapaxes(m + jnp.log(l), 2, 3)[..., 0]
    o = o.reshape(bq, nb * radius, h, dh)[:, :n]
    lse = lse.reshape(bq, nb * radius, h)[:, :n]
    return o, lse

def dilated_attention(q, k, v, rel_table):
    b, L, h, dh = q.shape
    outs, lses = [], []
    for window, dil in DILATED_PATTERNS:
        r = window // (2 * dil)
        n = L // dil

        def split(t):
            return t.reshape(b, n, dil, h, dh).transpose(0, 2, 1, 3, 4).reshape(b * dil, n, h, dh)

        rel = jnp.arange(3 * r)[None, :] - r - jnp.arange(r)[:, None]
        bias = rel_table[t5_bucket(rel * dil)].transpose(2, 0, 1).astype(jnp.float32)
        o, lse = banded_attention(split(q), split(k), split(v), bias, r)
        outs.append(o.reshape(b, dil, n, h, dh).transpose(0, 2, 1, 3, 4).reshape(b, L, h, dh))
        lses.append(lse.reshape(b, dil, n, h).transpose(0, 2, 1, 3).reshape(b, L, h))
    w = jax.nn.softmax(jnp.stack(lses, axis=0), axis=0)
    return jnp.einsum("pblh,pblhd->blhd", w, jnp.stack(outs, axis=0))

def ssd_scan(x, dt, a, bmat, cmat):
    b, L, g, hg, p = x.shape
    n = bmat.shape[-1]
    nc = L // CHUNK
    x = x.astype(jnp.float32)
    dt = dt.astype(jnp.float32)
    xc = (x * dt[..., None]).reshape(b, nc, CHUNK, g, hg, p)
    adt = (dt * a.astype(jnp.float32)).reshape(b, nc, CHUNK, g, hg)
    bc = bmat.astype(jnp.float32).reshape(b, nc, CHUNK, g, n)
    cc = cmat.astype(jnp.float32).reshape(b, nc, CHUNK, g, n)
    a_cs = jnp.cumsum(adt, axis=2)
    seg = a_cs[:, :, :, None] - a_cs[:, :, None, :]
    causal = jnp.tril(jnp.ones((CHUNK, CHUNK), dtype=bool))[None, None, :, :, None, None]
    decay = jnp.exp(jnp.where(causal, seg, -jnp.inf))
    cb = jnp.einsum("bclgn,bcsgn->bclsg", cc, bc)
    y_diag = jnp.einsum("bclsg,bclsgh,bcsghp->bclghp", cb, decay, xc)
    decay_states = jnp.exp(a_cs[:, :, -1:] - a_cs)
    states = jnp.einsum("bclgn,bclgh,bclghp->bcghpn", bc, decay_states, xc)
    chunk_decay = jnp.exp(a_cs[:, :, -1])

    def step(hstate, inp):
        s_c, d_c = inp
        return hstate * d_c[..., None, None] + s_c, hstate

    h0 = jnp.zeros((b, g, hg, p, n), jnp.float32)
    _, prev = lax.scan(step, h0, (jnp.moveaxis(states, 1, 0), jnp.moveaxis(chunk_decay, 1, 0)))
    prev = jnp.moveaxis(prev, 0, 1)
    y_off = jnp.einsum("bclgn,bcghpn,bclgh->bclghp", cc, prev, jnp.exp(a_cs))
    return (y_diag + y_off).reshape(b, L, g, hg, p)

def ssd_branch(z, xbc, dt_raw, conv_w, conv_b, dt_bias_f, dt_bias_b, a_log_f, a_log_b, d_skip, norm_g):
    b, L, _ = xbc.shape
    half = CONV_WIDTH // 2
    conv = lax.conv_general_dilated(xbc, conv_w[:, None, :], window_strides=(1,), padding=[(half, half)],
                                    dimension_numbers=("NWC", "WIO", "NWC"), feature_group_count=CONV_CH)
    xbc = jax.nn.silu(conv + conv_b)
    xs, bm, cm = jnp.split(xbc, [SSM_WIDTH, SSM_WIDTH + SSM_GROUPS * SSM_STATE], axis=-1)
    xs = xs.reshape(b, L, SSM_GROUPS, SSM_HEADS_PER_GROUP, SSM_HEAD_DIM)
    bm = bm.reshape(b, L, SSM_GROUPS, SSM_STATE)
    cm = cm.reshape(b, L, SSM_GROUPS, SSM_STATE)
    gh = (b, L, SSM_GROUPS, SSM_HEADS_PER_GROUP)
    dt_f = jax.nn.softplus((dt_raw[..., :SSM_HEADS] + dt_bias_f).astype(jnp.float32)).reshape(gh)
    dt_b = jax.nn.softplus((dt_raw[..., SSM_HEADS:] + dt_bias_b).astype(jnp.float32)).reshape(gh)
    a_f = -jnp.exp(a_log_f.astype(jnp.float32)).reshape(SSM_GROUPS, SSM_HEADS_PER_GROUP)
    a_b = -jnp.exp(a_log_b.astype(jnp.float32)).reshape(SSM_GROUPS, SSM_HEADS_PER_GROUP)
    y_f = ssd_scan(xs, dt_f, a_f, bm, cm)
    y_b = ssd_scan(xs[:, ::-1], dt_b[:, ::-1], a_b, bm[:, ::-1], cm[:, ::-1])[:, ::-1]
    y = y_f + y_b + d_skip.reshape(SSM_GROUPS, SSM_HEADS_PER_GROUP)[..., None] * xs
    y = y.reshape(b, L, SSM_WIDTH) * jax.nn.silu(z)
    y = rmsnorm(y.reshape(b, L, SSM_GROUPS, SSM_WIDTH // SSM_GROUPS), norm_g.reshape(SSM_GROUPS, -1))
    return y.reshape(b, L, SSM_WIDTH)

def hybrid_layer(x, pre_norm_g, w_in, rel_bias_table, attn_norm_g, conv_w, conv_b, dt_bias_fwd, dt_bias_bwd,
                 a_log_fwd, a_log_bwd, d_skip, ssm_norm_g, w_out, post_norm_g):
    b, L, _ = x.shape
    h = rmsnorm(x, pre_norm_g)
    proj = h @ w_in
    cuts = [ATTN_WIDTH, 2 * ATTN_WIDTH, 3 * ATTN_WIDTH, 4 * ATTN_WIDTH, 4 * ATTN_WIDTH + SSM_WIDTH,
            4 * ATTN_WIDTH + SSM_WIDTH + CONV_CH]
    q, k, v, z_attn, z_ssm, xbc, dt_raw = jnp.split(proj, cuts, axis=-1)
    hs = (b, L, ATTN_HEADS, ATTN_HEAD_DIM)
    o = dilated_attention(q.reshape(hs), k.reshape(hs), v.reshape(hs), rel_bias_table)
    attn_out = rmsnorm(o.reshape(b, L, ATTN_WIDTH), attn_norm_g) * jax.nn.silu(z_attn)
    ssm_out = ssd_branch(z_ssm, xbc, dt_raw, conv_w, conv_b, dt_bias_fwd, dt_bias_bwd, a_log_fwd, a_log_bwd,
                         d_skip, ssm_norm_g)
    mix = jnp.concatenate([attn_out.astype(x.dtype), ssm_out.astype(x.dtype)], axis=-1) @ w_out
    return (x + rmsnorm(mix, post_norm_g)).astype(x.dtype)

def setup_inputs(seed: int = 0) -> dict:
    key = jax.random.key(seed)
    ks = jax.random.split(key, 16)
    f32 = jnp.float32
    dt0 = jnp.exp(jax.random.uniform(ks[8], (DEPTH, SSM_HEADS), f32) * (math.log(0.1) - math.log(0.001))
                  + math.log(0.001))
    dt1 = jnp.exp(jax.random.uniform(ks[9], (DEPTH, SSM_HEADS), f32) * (math.log(0.1) - math.log(0.001))
                  + math.log(0.001))
    return {
        "x_prompt": jax.random.normal(ks[0], (BATCH, SEQ, D_MODEL), f32),
        "x_sample": jax.random.normal(ks[1], (DEC_BATCH, DEC_SEQ, D_MODEL), f32),
        "pre_norm_g": 1.0 + 0.1 * jax.random.normal(ks[2], (DEPTH, D_MODEL), f32),
        "w_in": jax.random.normal(ks[3], (DEPTH, D_MODEL, IN_COLS), f32) * D_MODEL ** -0.5,
        "rel_bias_table": 0.5 * jax.random.normal(ks[4], (N_BUCKETS, ATTN_HEADS), f32),
        "attn_norm_g": 1.0 + 0.1 * jax.random.normal(ks[5], (DEPTH, ATTN_WIDTH), f32),
        "conv_w": jax.random.normal(ks[6], (DEPTH, CONV_WIDTH, CONV_CH), f32) * CONV_WIDTH ** -0.5,
        "conv_b": 0.02 * jax.random.normal(ks[7], (DEPTH, CONV_CH), f32),
        "dt_bias_fwd": dt0 + jnp.log(-jnp.expm1(-dt0)),
        "dt_bias_bwd": dt1 + jnp.log(-jnp.expm1(-dt1)),
        "a_log_fwd": jnp.log(jax.random.uniform(ks[10], (DEPTH, SSM_HEADS), f32, 1.0, 16.0)),
        "a_log_bwd": jnp.log(jax.random.uniform(ks[11], (DEPTH, SSM_HEADS), f32, 1.0, 16.0)),
        "d_skip": 1.0 + 0.1 * jax.random.normal(ks[12], (DEPTH, SSM_HEADS), f32),
        "ssm_norm_g": 1.0 + 0.1 * jax.random.normal(ks[13], (DEPTH, SSM_WIDTH), f32),
        "w_out": jax.random.normal(ks[14], (DEPTH, MIX_WIDTH, D_MODEL), f32) * MIX_WIDTH ** -0.5,
        "post_norm_g": 1.0 + 0.1 * jax.random.normal(ks[15], (DEPTH, D_MODEL), f32),
    }

def reference(x_prompt, x_sample, pre_norm_g, w_in, rel_bias_table, attn_norm_g, conv_w, conv_b, dt_bias_fwd,
              dt_bias_bwd, a_log_fwd, a_log_bwd, d_skip, ssm_norm_g, w_out, post_norm_g):
    y_prompt = x_prompt
    y_sample = x_sample
    for i in range(DEPTH):
        y_prompt = hybrid_layer(y_prompt, pre_norm_g[i], w_in[i], rel_bias_table, attn_norm_g[i], conv_w[i],
                                conv_b[i], dt_bias_fwd[i], dt_bias_bwd[i], a_log_fwd[i], a_log_bwd[i], d_skip[i],
                                ssm_norm_g[i], w_out[i], post_norm_g[i])
        y_sample = hybrid_layer(y_sample, pre_norm_g[i], w_in[i], rel_bias_table, attn_norm_g[i], conv_w[i],
                                conv_b[i], dt_bias_fwd[i], dt_bias_bwd[i], a_log_fwd[i], a_log_bwd[i], d_skip[i],
                                ssm_norm_g[i], w_out[i], post_norm_g[i])
    return (y_prompt, y_sample)


_drawn_inputs = setup_inputs


def setup_inputs(seed=0):
    import zlib

    import numpy as np

    out = dict(_drawn_inputs(seed))
    spreads = {}
    factors = {'conv_b': 2.956}
    for name, (base, spread) in spreads.items():
        noise = np.random.default_rng([zlib.crc32(name.encode()), seed]).standard_normal(out[name].shape)
        drawn = base * np.exp(spread * noise) if base else spread * noise
        out[name] = __import__('jax').numpy.asarray(drawn.astype(out[name].dtype))
    for name, factor in factors.items():
        out[name] = (out[name] * factor).astype(out[name].dtype)
    return out
```

```python
import math
from contextlib import ExitStack

import numpy as np

import concourse.bass as bass
from concourse import mybir

P = 128
D_MODEL = 2048
SEQ, DEC_SEQ = 512, 256
T = SEQ + DEC_SEQ
HEADS, HEAD_DIM = 16, 128
WINDOWS = ((128, 1), (512, 4), (2048, 16))
N_BUCKETS, BUCKET_MAX_DIST = 32, 1024
SSM_HEADS, SSM_GROUPS = 32, 4
CONV_W = 5
EPS = 1e-6
NEG = -1e30

KT = D_MODEL // P
TT = T // P
PCH = SEQ // P
HALF_T = T // 2
KC = 4
NCH = KT // KC
SSM_TILES = 16
COL_Q, COL_K, COL_V, COL_ZA, COL_ZS, COL_XS, COL_B, COL_C, COL_DT = (
    0, 2048, 4096, 6144, 8192, 10240, 12288, 12800, 13312)
LOOP_COLS = (COL_V, COL_Q, COL_K, COL_ZA, COL_XS, COL_ZS)
V, Q, K, ZA, XS, ZS = range(6)
TILES = len(LOOP_COLS)
PRO_TILES = 2 * SSM_GROUPS + 1
PRO_CHUNKS = PRO_TILES * NCH
IT_CHUNKS = TILES * NCH
STRIP = SEQ + 3 * P
BROW = 1024

RUNS = []
for _d in range(2):
    for _first, _last in ((0, PCH), (PCH, TT)):
        for _lc in range(_first, _last):
            _src = range(_first, _lc) if _d == 0 else range(_lc + 1, _last)
            if len(_src):
                RUNS.append((_d, _lc, _src[0], len(_src), sum(r[3] for r in RUNS)))
PAIRS = sum(r[3] for r in RUNS)

GRP = 4
STEPS = 32 // GRP
STEP_GROUPS = (4, 5, 6, 7, 0, 1, 2, 3)
NB = 4
NBW = D_MODEL // NB
UNITS = STEPS * NB

DVE_PER_PASS = 28


def t5_bucket(rel):
    nb = N_BUCKETS // 2
    exact = nb // 2
    n = np.abs(rel)
    nf = np.maximum(n, 1).astype(np.float32)
    large = exact + (np.log(nf / np.float32(exact)) / np.float32(math.log(BUCKET_MAX_DIST / exact))
                     * np.float32(nb - exact)).astype(np.int32)
    return np.where(rel > 0, nb, 0) + np.where(n < exact, n, np.minimum(large, nb - 1))


def shape_constants():
    k, s = np.arange(P)[:, None], np.arange(P)[None]
    sq = np.concatenate([k == s, k <= s, k >= s, k > s, k < s, np.ones((P, P))], 1).astype(np.float32)
    rel = np.arange(BROW) - (SEQ - 1)
    count = sum(((rel % dil == 0) & (np.abs(rel) <= win // 2)).astype(np.int64) for win, dil in WINDOWS)
    hot = np.zeros((N_BUCKETS + 1, BROW), np.float32)
    hot[t5_bucket(rel), np.arange(BROW)] = 1.0
    hot[N_BUCKETS] = np.where(count > 0, np.log(np.maximum(count, 1)), NEG)
    return sq, hot


def encoder(nc, x_prompt, x_sample, pre_g, w_in, rel_table, attn_g, conv_w, conv_b, dtb_f, dtb_b,
            alog_f, alog_b, d_skip, ssm_g, w_out, post_g, squares, hots,
            u_scr, brow_scr, strip_scr, loc_scr, er_scr, cb_scr, y_prompt, y_sample):
    f32, f32r = mybir.dt.float32, mybir.dt.float32r
    ALU, ACT, AX = mybir.AluOpType, mybir.ActivationFunctionType, mybir.AxisListType
    ds = bass.ds

    ctx = ExitStack()
    with ctx:
        def sb(name, shape, dt=f32):
            return ctx.enter_context(nc.sbuf_tensor(name, shape, dt))

        def sem(name):
            return ctx.enter_context(nc.semaphore(name))

        h_hi = sb("h_hi", [P, KT * T], f32r)
        h_lo = sb("h_lo", [P, KT * T], f32r)
        w_raw = sb("w_raw", [P, NCH, KC * P])
        w_hi = sb("w_hi", [P, NCH, KC * P], f32r)
        w_lo = sb("w_lo", [P, NCH, KC * P], f32r)
        sq_c = sb("sq_c", [P, 6 * P])
        ident, tri_f, tri_b, stri_f, stri_b, ones = (sq_c[:, i * P:(i + 1) * P] for i in range(6))
        tri_incl, tri_strict = (tri_f, tri_b), (stri_f, stri_b)
        conv_cols = sb("conv_cols", [P, CONV_W * 24])
        vec_cols = sb("vec_cols", [P, 72])
        convb_cols, pre_cols, mix_cols = vec_cols[:, 0:24], vec_cols[:, 24:40], vec_cols[:, 40:72]
        skip_cols = sb("skip_cols", [P, SSM_TILES])
        loc_dt = sb("loc_dt", [P, 2 * TT * 64])
        loc_cols, dt_cols = loc_dt[:, 0:TT * 64], loc_dt[:, TT * 64:]
        coef = sb("coef", [P, PAIRS * 32])
        osq_sum = sb("osq_sum", [P, T])
        cur = sb("cur", [P, 128])
        tap_cur, bias_cur, skip_cur = cur[:, 0:5], cur[:, 5:6], cur[:, 6:7]
        coef_cur, loc_cur, dt_cur = cur[:, 8:36], cur[:, 36:60], cur[:, 60:84]
        mx, nmx, lsum, rinv = (cur[:, 84 + 6 * i:90 + 6 * i] for i in range(4))
        ssq, rx = cur[:, 108:114], cur[:, 114:120]
        stage = sb("stage", [P, 22528])
        at = [0]

        def carve(n):
            at[0] += n
            assert at[0] <= 22528
            return stage[:, at[0] - n:at[0]]

        XW = T + 8
        xs_raw = carve(XW)
        qT, kT, vT, v_tok, za, xsT, zs = (carve(T) for _ in range(7))
        strip = carve(STRIP)
        probs = carve(4 * SEQ)
        probs_s = carve(2 * DEC_SEQ)
        pT = carve(4 * SEQ)
        pT_s = carve(2 * DEC_SEQ)
        oT = carve(T)
        sqT = carve(XW)
        decay = carve(4 * T)
        er = carve(2 * T)
        cb = carve(PAIRS * P + 2 * T)
        x_tok = carve(T)
        conv = sqT
        xsc = pT[:, 0:PAIRS * P]
        y, ytmp = probs[:, 0:T], probs[:, T:2 * T]
        x_rows = [stage[:, t * D_MODEL:(t + 1) * D_MODEL] for t in range(TT)]
        x_junk = stage[:, TT * D_MODEL:(TT + 1) * D_MODEL]
        s0 = (TT + 1) * D_MODEL
        par_a, par_b = stage[0:120, s0:s0 + P], stage[0:72, s0 + P:s0 + 2 * P]
        table = stage[0:33, s0 + 2 * P:s0 + 2 * P + 16]
        hot = stage[0:33, s0 + 512:s0 + 512 + BROW]
        brow = stage[0:16, s0 + 2048:s0 + 2048 + BROW]
        bc_raw = [decay[:, 0:XW], decay[:, XW:2 * XW]]
        bc_conv = [decay[:, 2 * XW:3 * XW], er[:, 0:XW]]
        bcT = [probs[:, 0:T], probs[:, T:2 * T]]
        dtT = pT[0:64, 0:T]
        W6 = TT * 64
        dx, du, dz, dz2, dp = (pT[:, T:T + W6], pT[:, T + W6:T + 2 * W6], pT[:, T + 2 * W6:T + 3 * W6],
                               probs_s[:, 0:W6], pT_s[:, 0:W6])
        adt = oT[:, 0:W6]
        dtb_row, a_row = sqT[:, 0:64], sqT[:, 64:128]
        loc_rows, er_rows = x_tok[0:64, :], er[0:64, XW - 16:XW - 16 + T]
        er_rows = oT[0:64, 0:T]
        adt = sqT[:, 128:128 + W6]

        MG = GRP * T
        m_hi = [h_hi[:, i * MG:(i + 1) * MG] for i in range(2)]
        m_lo = [h_lo[:, i * MG:(i + 1) * MG] for i in range(2)]
        WG = GRP * NBW
        w2_hi = [h_hi[:, 2 * MG + i * WG:2 * MG + (i + 1) * WG] for i in range(2)]
        w2_lo = [h_lo[:, 2 * MG + i * WG:2 * MG + (i + 1) * WG] for i in range(2)]
        acc = stage[:, 0:TT * D_MODEL]
        w2_raw = [stage[:, TT * D_MODEL + i * WG:TT * D_MODEL + (i + 1) * WG] for i in range(2)]
        u_raw = stage[:, TT * D_MODEL + 2 * WG:TT * D_MODEL + 2 * WG + MG]
        usq = stage[:, TT * D_MODEL + 2 * WG + MG:TT * D_MODEL + 2 * WG + 2 * MG]
        ssum = loc_dt[:, :]
        g_row = w_raw[:, :, :].rearrange("p a b -> p (a b)")
        x_back = [stage[:, TT * D_MODEL + i * D_MODEL:TT * D_MODEL + (i + 1) * D_MODEL] for i in range(3)]
        r_cur = sb("r_cur", [P, 2, TT])
        fin = sb("fin", [P, 3, TT])

        ps = ctx.enter_context(nc.psum_tensor("ps", [P, 8, 512], f32))

        x_in = [sem(f"x_in{t}") for t in range(TT)]
        small_in, hot_in, brow_out, strip_out = sem("small_in"), sem("hot_in"), sem("brow_out"), sem("strip_out")
        row_in = sem("row_in")
        x_squared, x_ms, x_root, x_rinv, x_scaled = (sem(n) for n in (
            "x_squared", "x_ms", "x_root", "x_rinv", "x_scaled"))
        cols_ready, cols_read, brow_ready, brow_read = (sem(n) for n in (
            "cols_ready", "cols_read", "brow_ready", "brow_read"))
        table_ones = sem("table_ones")
        xt_done, h_hi_done, h_lo_done = sem("xt_done"), sem("h_hi_done"), sem("h_lo_done")
        w_in_s = [sem(f"w_in{c}") for c in range(NCH)]
        w_hi_done, w_lo_done, w_used = sem("w_hi_done"), sem("w_lo_done"), sem("w_used")
        tile_done, tile_out = sem("tile_done"), sem("tile_out")
        pads = sem("pads")
        bc_conved, bc_silu, pcb_ready, pcb_read, cb_stored = (sem(n) for n in (
            "bc_conved", "bc_silu", "pcb_ready", "pcb_read", "cb_stored"))
        dt_out, dtt_ready, dt_exp_arg, dt_exp, a_exp, adt_ready = (sem(n) for n in (
            "dt_out", "dtt_ready", "dt_exp_arg", "dt_exp", "a_exp", "adt_ready"))
        cum_ready, loc_read, rows_read, coef_exp, coef_done = (sem(n) for n in (
            "cum_ready", "loc_read", "rows_read", "coef_exp", "coef_done"))
        rows_stored = sem("rows_stored")
        strip_in, decay_in, er_in, cb_in = sem("strip_in"), sem("decay_in"), sem("er_in"), sem("cb_in")
        scores_ready, sscores_ready, pt_ready, pts_ready, pv_ready, vt_ready = (sem(n) for n in (
            "scores_ready", "sscores_ready", "pt_ready", "pts_ready", "pv_ready", "vt_ready"))
        biased, negmax, probs_exp, normed, pt_out_act, pt_out_dve, pts_out = (sem(n) for n in (
            "biased", "negmax", "probs_exp", "normed", "pt_out_act", "pt_out_dve", "pts_out"))
        o_out, o_sq, att_gated, ua_stored, vt_out = (sem(n) for n in (
            "o_out", "o_sq", "att_gated", "ua_stored", "vt_out"))
        conved, xs_silu, xt_ready, xt_out, xsc_done, decay_arg, decay_exp, wmat_done = (sem(n) for n in (
            "conved", "xs_silu", "xt_ready", "xt_out", "xsc_done", "decay_arg", "decay_exp", "wmat_done"))
        off_ready, off_read, diag_ready, y_gated, ys_stored = (sem(n) for n in (
            "off_ready", "off_read", "diag_ready", "y_gated", "ys_stored"))
        dve_seq = sem("dve_seq")
        u_in, w2_in = sem("u_in"), [sem(f"w2_in{i}") for i in range(2)]
        g_in = sem("g_in")
        usq_done, m_hi_done, m_lo_done, w2_hi_done, w2_lo_done = (sem(n) for n in (
            "usq_done", "m_hi_done", "m_lo_done", "w2_hi_done", "w2_lo_done"))
        ssum_ready, stat_ready, stat_read, r_root, r_ready, part_ready, acc_added = (sem(n) for n in (
            "ssum_ready", "stat_ready", "stat_read", "r_root", "r_ready", "part_ready", "acc_added"))
        xb_in = [sem(f"xb_in{i}") for i in range(3)]
        fin_sq, fin_ms, fin_root, fin_done, y_out = (sem(n) for n in (
            "fin_sq", "fin_ms", "fin_root", "fin_done", "y_out"))

        w_rows = w_in[0].rearrange("(k p) n -> p k n", p=P)
        w2_rows = w_out[0].rearrange("(k p) n -> p k n", p=P)
        chunk_of = lambda i, m: PRO_CHUNKS + IT_CHUNKS * i + m
        tile_of = lambda i, j: PRO_TILES + TILES * i + j
        block = ctx.enter_context(nc.Block())

        @block.sync
        def _(sp):
            sp.dma_start(sq_c[:, :], squares).then_inc(small_in, 16)
            sp.dma_start(par_a, conv_w[0].rearrange("k (t p) -> (k t) p", p=P)).then_inc(small_in, 16)
            r = 0
            for v in (conv_b, pre_g, attn_g, ssm_g):
                n = v.shape[1] // P
                sp.dma_start(par_b[r:r + n, :], v[0].rearrange("(t p) -> t p", p=P)).then_inc(small_in, 16)
                r += n
            for t in range(TT):
                src = x_prompt[0, t * P:(t + 1) * P, :] if t < PCH else x_sample[0, (t - PCH) * P:(t - PCH + 1) * P, :]
                sp.dma_start(x_rows[t], src).then_inc(x_in[t], 16)
            sp.dma_start(table[0:32, :], rel_table).then_inc(hot_in, 16)
            sp.dma_start(hot, hots).then_inc(hot_in, 16)

            def load_w(n, col, c, width=P, waited=False):
                src = w_rows[:, c * KC:(c + 1) * KC, ds(col, width)]
                if not waited and (not isinstance(n, int) or n >= NCH):
                    sp.wait_ge(w_lo_done, n - NCH + 1)
                sp.dma_start(w_raw[:, c, :].rearrange("p (k n) -> p k n", k=KC)[:, :, 0:width], src
                             ).then_inc(w_in_s[c], 16)

            for c in range(NCH):
                load_w(c, COL_B, c)
            for c in range(NCH):
                load_w(NCH + c, COL_C, c)
            sp.wait_ge(brow_read, 2)
            sp.dma_start(brow_scr, brow).then_inc(brow_out, 16)
            sp.wait_ge(brow_out, 16)
            sp.dma_start(strip_scr, bass.AP(brow_scr.tensor, P - 1, [[BROW, HEADS], [-1, P], [1, STRIP]])
                         ).then_inc(strip_out, 16)
            sp.wait_ge(xt_done, KT)
            for q, v in enumerate((dtb_f, dtb_b)):
                sp.dma_start(dtb_row[:, 32 * q:32 * q + 32], v.partition_broadcast(P).rearrange("p a b -> p (a b)")
                             ).then_inc(row_in, 16)
            for q, v in enumerate((alog_f, alog_b)):
                sp.dma_start(a_row[:, 32 * q:32 * q + 32], v.partition_broadcast(P).rearrange("p a b -> p (a b)")
                             ).then_inc(row_in, 16)
            with sp.Fori(1, SSM_GROUPS) as g:
                gcol = sp.snap(g * P)
                for j, base in enumerate((COL_B, COL_C)):
                    for c in range(NCH):
                        load_w(2 * NCH * g + NCH * j + c, gcol + base, c)
            for c in range(NCH):
                load_w(2 * NCH * SSM_GROUPS + c, COL_DT, c, width=64)

            def reload(a):
                sp.dma_start(decay.rearrange("p (d n) -> p d n", d=2),
                             loc_scr.rearrange("(d h) t -> d (h t)", d=2)[:, ds(a * 2 * T, 2 * T)]
                             .partition_broadcast(P)).then_inc(decay_in, 16)
                for h in range(2):
                    sp.dma_start(er[64 * h:64 * h + 64, :].rearrange("p (d n) -> p d n", d=2),
                                 er_scr.rearrange("(d h) t -> d (h t)", d=2)[:, ds(a * 2 * T + h * T, T)]
                                 .partition_broadcast(64)).then_inc(er_in, 16)
                sp.dma_start(cb, cb_scr[ds((a // 4) * P, P), :]).then_inc(cb_in, 16)

            def load_strip(i):
                if not isinstance(i, int):
                    sp.wait_ge(biased, 6 * i)
                sp.dma_start(strip, strip_scr[ds(i * P, P), :]).then_inc(strip_in, 16)

            def iteration(i, a):
                for m in range(IT_CHUNKS):
                    j, c = divmod(m, NCH)
                    if m == NCH and a is not None:
                        sp.wait_ge(w_lo_done, chunk_of(i, m) - NCH + 1)
                        reload(a)
                        load_w(chunk_of(i, m), i * P + LOOP_COLS[j], c, waited=True)
                    else:
                        load_w(chunk_of(i, m), i * P + LOOP_COLS[j], c)
                    if m == 15:
                        load_strip(i)

            for m in range(16):
                j, c = divmod(m, NCH)
                load_w(chunk_of(0, m), LOOP_COLS[j], c)
            sp.wait_ge(strip_out, 16)
            load_strip(0)
            for m in range(16, IT_CHUNKS):
                j, c = divmod(m, NCH)
                load_w(chunk_of(0, m), LOOP_COLS[j], c)
            sp.wait_ge(rows_stored, 32)
            sp.wait_ge(cb_stored, 16 * SSM_GROUPS)
            with sp.Fori(0, HEADS - 1) as a:
                iteration(a + 1, a)
            sp.wait_ge(y_gated, HEADS - 1)
            reload(HEADS - 1)

            sp.wait_ge(ua_stored, 16 * HEADS)
            sp.wait_ge(ys_stored, 16 * SSM_TILES)

            def load_u(s):
                if s:
                    sp.wait_ge(m_lo_done, GRP * s)
                    sp.wait_ge(ssum_ready, s)
                g0 = STEP_GROUPS[s] * GRP
                sp.dma_start(u_raw.rearrange("p (k t) -> p k t", k=GRP),
                             u_scr[g0 * P:(g0 + GRP) * P, :].rearrange("(k p) t -> p k t", p=P)).then_inc(u_in, 16)

            def load_w2(u):
                if u >= 2:
                    sp.wait_ge(w2_lo_done, u - 1)
                s, nb = divmod(u, NB)
                k0 = STEP_GROUPS[s] * GRP
                sp.dma_start(w2_raw[u % 2].rearrange("p (k n) -> p k n", k=GRP),
                             w2_rows[:, k0:k0 + GRP, nb * NBW:(nb + 1) * NBW]).then_inc(w2_in[u % 2], 16)

            load_u(0)
            sp.dma_start(g_row, post_g.partition_broadcast(P).rearrange("p a b -> p (a b)")).then_inc(g_in, 16)
            for u in range(UNITS):
                load_w2(u)
                if u % NB == 2 and u // NB + 1 < STEPS:
                    load_u(u // NB + 1)
            sp.wait_ge(w2_lo_done, UNITS)
            sp.wait_ge(m_lo_done, GRP * STEPS)

            def x_src(t):
                return x_prompt[0, t * P:(t + 1) * P, :] if t < PCH else x_sample[0, (t - PCH) * P:(t - PCH + 1) * P, :]
            for t in range(3):
                sp.dma_start(x_back[t], x_src(t)).then_inc(xb_in[t], 16)
            for t in range(TT):
                sp.wait_ge(fin_done, t + 1)
                dst = y_prompt[0, t * P:(t + 1) * P, :] if t < PCH else y_sample[0, (t - PCH) * P:(t - PCH + 1) * P, :]
                sp.dma_start(dst, acc[:, t * D_MODEL:(t + 1) * D_MODEL]).then_inc(y_out, 16)
                if t + 3 < TT:
                    sp.dma_start(x_back[t], x_src(t + 3)).then_inc(xb_in[t], 16)
            sp.wait_ge(y_out, 16 * TT)

        @block.tensor
        def _(pe):
            pe.wait_ge(small_in, 16 * 6)
            nc.tensor.transpose(ps[:, 0, 0:120], par_a, ident[0:120, 0:120])
            nc.tensor.transpose(ps[:, 0, 128:200], par_b, ident[0:72, 0:72]).then_inc(cols_ready, 1)
            pe.wait_ge(hot_in, 32)
            pe.wait_ge(table_ones, 1)
            for n in range(2):
                nc.tensor.matmul(ps[0:16, 1 + n, :], table, hot[:, n * 512:(n + 1) * 512],
                                 start=True, stop=True).then_inc(brow_ready, 1)
            pe.wait_ge(x_scaled, TT)
            pe.wait_ge(cols_read, 2)
            pe.wait_ge(brow_read, 2)
            for k in range(KT):
                if k >= 4:
                    pe.wait_ge(h_lo_done, k - 3)
                for t in range(TT):
                    last = nc.tensor.transpose(ps[:, 2 * (k % 4) + t // 3, (t % 3) * P:(t % 3 + 1) * P],
                                               x_rows[t][:, k * P:(k + 1) * P], ident)
                last.then_inc(xt_done, 1)

            def gemm_half(n, tile, parity, half):
                if half == 0 and (not isinstance(tile, int) or tile >= 2):
                    pe.wait_ge(tile_out, tile - 1)
                for c in (2 * half, 2 * half + 1):
                    pe.wait_ge(w_lo_done, n + c + 1)
                    for kk in range(KC):
                        k = c * KC + kk
                        w_h, w_l = (w[:, c, kk * P:(kk + 1) * P] for w in (w_hi, w_lo))
                        for p, (w, h) in enumerate(((w_h, h_hi), (w_h, h_lo), (w_l, h_hi))):
                            for b in range(2):
                                last = nc.tensor.matmul(
                                    ps[:, 2 * parity + b, 0:HALF_T], w,
                                    h[:, k * T + b * HALF_T:k * T + (b + 1) * HALF_T],
                                    start=(k == 0 and p == 0), stop=(k == KT - 1 and p == 2))
                                if k == KT - 1 and p == 2 and b == 1:
                                    last.then_inc(tile_done, 1)
                                    last = None
                    if last is not None:
                        last.then_inc(w_used, 1)

            def cb_prompt(g):
                pe.wait_ge(bc_silu, 2 * g + 2)
                for sc in range(PCH):
                    nc.tensor.matmul(ps[:, 4 + sc, :], bcT[0][:, sc * P:(sc + 1) * P], bcT[1][:, 0:SEQ],
                                     start=True, stop=True).then_inc(pcb_ready, 1)

            def cb_sample(g):
                pe.wait_ge(pcb_read, 5 * g + 1)
                for q in range(2):
                    last = nc.tensor.matmul(ps[:, 4, q * DEC_SEQ:(q + 1) * DEC_SEQ],
                                            bcT[0][:, SEQ + q * P:SEQ + (q + 1) * P], bcT[1][:, SEQ:T],
                                            start=True, stop=True)
                last.then_inc(pcb_ready, 1)

            def bc_tiles(g, post):
                for half in range(4):
                    gemm_half(2 * NCH * g + NCH * (half // 2), 2 * g + half // 2, half // 2, half % 2)
                    if post is not None and half == 2:
                        cb_prompt(post)
                    if post is not None and half == 3:
                        cb_sample(post)

            pe.wait_ge(h_lo_done, KT)
            bc_tiles(0, None)
            with pe.Fori(0, SSM_GROUPS - 1) as g:
                bc_tiles(g + 1, g)
            for half in range(2):
                gemm_half(2 * NCH * SSM_GROUPS, PRO_TILES - 1, 0, half)
            cb_prompt(SSM_GROUPS - 1)
            cb_sample(SSM_GROUPS - 1)

            def dt_transposes():
                pe.wait_ge(dt_out, 1)
                pe.wait_ge(pcb_read, 5 * (SSM_GROUPS - 1) + 2)
                for c in range(TT):
                    last = nc.tensor.transpose(ps[:, 5, c * 64:(c + 1) * 64], dtT[:, c * P:(c + 1) * P],
                                               ident[0:64, 0:64])
                last.then_inc(dtt_ready, 1)

            def dt_cumulate():
                pe.wait_ge(adt_ready, 1)
                pe.wait_ge(pcb_read, 5 * SSM_GROUPS)
                adt3 = adt.rearrange("p (c n) -> p c n", c=TT)
                loc3 = ps[:, 4, 0:W6].rearrange("p (c n) -> p c n", c=TT)
                for d in range(2):
                    last = nc.tensor.matmul(loc3[:, :, 32 * d:32 * d + 32], tri_incl[d],
                                            adt3[:, :, 32 * d:32 * d + 32], start=(d == 0), stop=True,
                                            skip_group_check=True)
                last.then_inc(cum_ready, 1)
                for c in range(TT):
                    for d in range(2):
                        b, o = (5, c) if c < PCH else (6, c - PCH)
                        last = nc.tensor.matmul(ps[32 * d:32 * d + 32, b, o * P:(o + 1) * P],
                                                adt3[:, c, 32 * d:32 * d + 32], tri_incl[d],
                                                start=True, stop=True)
                last.then_inc(cum_ready, 1)
                for d, lc, sc0, n, pair0 in RUNS:
                    for q in range(n):
                        sc = sc0 + q
                        out = ps[:, 7, (pair0 + q) * 32:(pair0 + q + 1) * 32]
                        mids = range(sc + 1, lc) if d == 0 else range(lc + 1, sc)
                        last = nc.tensor.matmul(out, tri_strict[d], adt3[:, sc, 32 * d:32 * d + 32],
                                                start=True, stop=(len(mids) == 0))
                        for m in mids:
                            last = nc.tensor.matmul(out, ones, adt3[:, m, 32 * d:32 * d + 32],
                                                    start=False, stop=(m == mids[-1]))
                last.then_inc(cum_ready, 1)

            def slot(s, a, i):
                if a is not None and s == 0:
                    pe.wait_ge(tile_out, PRO_TILES + TILES * a + K + 1)
                    pe.wait_ge(vt_out, 2 * a + 2)
                    for t in range(PCH):
                        nc.tensor.matmul(ps[:, 4 + t, :], qT[:, t * P:(t + 1) * P], kT[:, 0:SEQ],
                                         start=True, stop=True).then_inc(scores_ready, 1)
                if a is not None and s == 1:
                    pe.wait_ge(biased, 6 * a + 1)
                    for t in range(2):
                        last = nc.tensor.matmul(ps[:, 4, t * DEC_SEQ:(t + 1) * DEC_SEQ],
                                                qT[:, SEQ + t * P:SEQ + (t + 1) * P], kT[:, SEQ:T],
                                                start=True, stop=True)
                    last.then_inc(sscores_ready, 1)
                if a is not None and s == 2:
                    pe.wait_ge(normed, 6 * a + 4)
                    pe.wait_ge(biased, 6 * a + 6)
                    for b in range(PCH):
                        for t in range(PCH):
                            last = nc.tensor.transpose(ps[:, 4 + b, t * P:(t + 1) * P],
                                                       probs[:, t * SEQ + b * P:t * SEQ + (b + 1) * P], ident)
                        last.then_inc(pt_ready, 1)
                if a is not None and s == 3:
                    pe.wait_ge(normed, 6 * a + 6)
                    pe.wait_ge(pt_out_act, 2 * a + 1)
                    for b in range(2):
                        for t in range(2):
                            o = b * DEC_SEQ
                            last = nc.tensor.transpose(
                                ps[:, 4, o + t * P:o + (t + 1) * P],
                                probs_s[:, t * DEC_SEQ + b * P:t * DEC_SEQ + (b + 1) * P], ident)
                    last.then_inc(pts_ready, 1)
                if a is not None and s == 4:
                    pe.wait_ge(pt_out_act, 2 * a + 2)
                    pe.wait_ge(pt_out_dve, 2 * a + 2)
                    for b in range(PCH):
                        last = nc.tensor.matmul(ps[:, 5, :], v_tok[:, b * P:(b + 1) * P],
                                                pT[:, b * SEQ:(b + 1) * SEQ], start=(b == 0), stop=(b == PCH - 1))
                    last.then_inc(pv_ready, 1)
                    pe.wait_ge(pts_out, a + 1)
                    for b in range(2):
                        last = nc.tensor.matmul(ps[:, 6, 0:DEC_SEQ], v_tok[:, SEQ + b * P:SEQ + (b + 1) * P],
                                                pT_s[:, b * DEC_SEQ:(b + 1) * DEC_SEQ],
                                                start=(b == 0), stop=(b == 1))
                    last.then_inc(pv_ready, 1)
                if a is not None and s == 5:
                    pe.wait_ge(xs_silu, a + 1)
                    for half, bank in ((0, 7), (1, 4)):
                        for q in range(3):
                            c = 3 * half + q
                            last = nc.tensor.transpose(ps[:, bank, q * P:(q + 1) * P],
                                                       xsT[:, c * P:(c + 1) * P], ident)
                        last.then_inc(xt_ready, 1)
                if a is not None and s == 7:
                    pe.wait_ge(o_out, 2 * a + 2)
                    pe.wait_ge(xsc_done, a + 1)
                    pe.wait_ge(cb_in, 16 * a + 16)
                    for d, (bp, bs) in enumerate(((5, 6), (7, 4))):
                        for rd, lc, sc0, n, pair0 in RUNS:
                            if rd != d:
                                continue
                            b, o = (bp, lc) if lc < PCH else (bs, lc - PCH)
                            for q in range(n):
                                pr = pair0 + q
                                last = nc.tensor.matmul(ps[:, b, o * P:(o + 1) * P], xsc[:, pr * P:(pr + 1) * P],
                                                        cb[:, pr * P:(pr + 1) * P], start=(q == 0),
                                                        stop=(q == n - 1))
                        last.then_inc(off_ready, 1)
                if a is not None and s == 9:
                    pe.wait_ge(off_read, 2 * a + 1)
                    pe.wait_ge(wmat_done, a + 1)
                    for c in range(TT):
                        b, o = (5, c) if c < PCH else (6, c - PCH)
                        for h in range(2):
                            last = nc.tensor.matmul(
                                ps[64 * h:64 * h + 64, b, o * P:(o + 1) * P],
                                x_tok[:, c * P + 64 * h:c * P + 64 * h + 64],
                                decay[:, h * T + c * P:h * T + (c + 1) * P], start=True, stop=True)
                        if c in (PCH - 1, TT - 1):
                            last.then_inc(diag_ready, 1)
                if a is not None and s == 11:
                    pe.wait_ge(y_gated, a + 1)
                if i is not None and s == 10:
                    pe.wait_ge(tile_out, tile_of(i, V) + 1)
                    if a is not None:
                        pe.wait_ge(off_read, 2 * a + 2)
                    else:
                        pe.wait_ge(coef_exp, 1)
                        pe.wait_ge(loc_read, 1)
                    for half, bank in ((0, 7), (1, 4)):
                        for q in range(3):
                            c = 3 * half + q
                            last = nc.tensor.transpose(ps[:, bank, q * P:(q + 1) * P],
                                                       vT[:, c * P:(c + 1) * P], ident)
                        last.then_inc(vt_ready, 1)

            def iteration(i, a):
                for s in range(2 * TILES):
                    j, half = divmod(s, 2)
                    gemm_half(chunk_of(i, NCH * j), tile_of(i, j), (1 + j) % 2, half)
                    if a is None and s == 0:
                        dt_transposes()
                    if a is None and s == 4:
                        dt_cumulate()
                    slot(s, a, i)

            iteration(0, None)
            with pe.Fori(0, HEADS - 1) as a:
                iteration(a + 1, a)
            for s in range(2 * TILES):
                slot(s, HEADS - 1, None)

            with pe.Fori(0, STEPS // 2) as pair:
                for par in range(2):
                    step = pair * 2 + par
                    pe.wait_ge(ssum_ready, step + 1)
                    for t in range(TT):
                        last = nc.tensor.matmul(ps[:, 6, t:t + 1], ssum[:, t * P:(t + 1) * P], ones[:, 0:1],
                                                start=True, stop=True)
                    last.then_inc(stat_ready, 1)
                    pe.wait_ge(m_lo_done, GRP * step + GRP)
                    for nb in range(NB):
                        unit = pair * (2 * NB) + (par * NB + nb)
                        pe.wait_ge(w2_lo_done, unit + 1)
                        for t in range(TT):
                            pe.wait_ge(acc_added, unit * TT + (t + 1))
                            for k in range(GRP):
                                for p, (m, w) in enumerate(((m_hi, w2_hi), (m_hi, w2_lo), (m_lo, w2_hi))):
                                    last = nc.tensor.matmul(
                                        ps[:, t, :], m[par][:, k * T + t * P:k * T + (t + 1) * P],
                                        w[nb % 2][:, k * NBW:(k + 1) * NBW],
                                        start=(k == 0 and p == 0), stop=(k == GRP - 1 and p == 2))
                            last.then_inc(part_ready, 1)

        @block.scalar
        def _(act):
            for t in range(TT):
                act.wait_ge(x_in[t], 16)
                if t:
                    act.wait_ge(x_squared, t)
                nc.scalar.activation(x_junk, x_rows[t], ACT.Square, accum_out=ssq[:, t:t + 1]).then_inc(x_squared, 1)
            act.wait_ge(x_ms, 1)
            nc.scalar.activation(rx, ssq, ACT.Sqrt).then_inc(x_root, 1)
            for h in range(2):
                act.dma_start(skip_cols[64 * h:64 * h + 64, :],
                              d_skip[0].rearrange("(t h) -> h t", h=2)[h:h + 1, :].partition_broadcast(64)
                              .rearrange("p a b -> p (a b)"), allow_slow_non_contiguous=True).then_inc(small_in, 16)

            def split_hi(n, c, tile):
                act.wait_ge(w_in_s[c], 16 * tile + 16)
                if not isinstance(n, int) or n >= NCH:
                    if c == NCH - 1:
                        act.wait_ge(tile_done, tile)
                    else:
                        act.wait_ge(w_used, tile * (NCH - 1) + (c + 2 - NCH))
                nc.scalar.activation(w_hi[:, c, :], w_raw[:, c, :], ACT.Copy).then_inc(w_hi_done, 1)

            def tile_ready(tile):
                act.wait_ge(tile_done, tile + 1)

            def tile_into(tile, parity, dst, func=ACT.Copy, scale=1.0):
                nc.scalar.activation(dst.rearrange("p (b t) -> p b t", b=2),
                                     ps[:, 2 * parity:2 * parity + 2, 0:HALF_T], func, scale=scale
                                     ).then_inc(tile_out, 1)

            def tile_padded(parity, dst):
                nc.scalar.activation(dst[:, 2:2 + HALF_T], ps[:, 2 * parity, 0:HALF_T], ACT.Copy)
                nc.scalar.activation(dst[:, 2 + HALF_T:2 + SEQ], ps[:, 2 * parity + 1, 0:SEQ - HALF_T], ACT.Copy)
                nc.scalar.activation(dst[:, 6 + SEQ:6 + T], ps[:, 2 * parity + 1, SEQ - HALF_T:HALF_T], ACT.Copy
                                     ).then_inc(tile_out, 1)

            def silu(dst, src, done):
                nc.scalar.activation(dst[:, 0:SEQ], src[:, 0:SEQ], ACT.Silu)
                nc.scalar.activation(dst[:, SEQ:T], src[:, SEQ + 4:T + 4], ACT.Silu).then_inc(done, 1)

            act.wait_ge(cols_read, 2)
            for k in range(KT):
                act.wait_ge(xt_done, k + 1)
                nc.scalar.activation(h_hi[:, k * T:(k + 1) * T].rearrange("p (b t) -> p b t", b=2),
                                     ps[:, 2 * (k % 4):2 * (k % 4) + 2, 0:HALF_T], ACT.Copy,
                                     scale=pre_cols[:, k:k + 1]).then_inc(h_hi_done, 1)
                if k >= KT - NCH:
                    split_hi(k - (KT - NCH), k - (KT - NCH), 0)

            def bc_steps(g, post):
                for s in range(4):
                    for m in (2 * s + 4, 2 * s + 5):
                        split_hi(2 * NCH * g + m, m % NCH, 2 * g + m // NCH)
                    if s == 1:
                        tile_ready(2 * g)
                        if post is not None:
                            act.wait_ge(bc_conved, 2 * post + 1)
                        else:
                            act.wait_ge(pads, 2)
                        tile_padded(0, bc_raw[0])
                        if post is not None:
                            silu(bcT[0], bc_conv[0], bc_silu)
                            act.wait_ge(bc_conved, 2 * post + 2)
                            silu(bcT[1], bc_conv[1], bc_silu)
                    if s == 3:
                        tile_ready(2 * g + 1)
                        tile_padded(1, bc_raw[1])
                        if post is not None:
                            store_cb(post)

            def store_cb(g):
                act.wait_ge(pcb_read, 5 * g + 5)
                act.dma_start(cb_scr[ds(g * P, P), :], cb).then_inc(cb_stored, 16)
                act.wait_ge(cb_stored, 16 * g + 16)

            bc_steps(0, None)
            with act.Fori(0, SSM_GROUPS - 1) as g:
                bc_steps(g + 1, g)
            last = SSM_GROUPS - 1
            dt_n = 2 * NCH * SSM_GROUPS
            for s in range(2):
                for m in (2 * s + 4, 2 * s + 5):
                    split_hi(dt_n + m, m % NCH, PRO_TILES - 1 + m // NCH)
                if s == 1:
                    act.wait_ge(bc_conved, 2 * last + 1)
                    silu(bcT[0], bc_conv[0], bc_silu)
                    act.wait_ge(bc_conved, 2 * last + 2)
                    silu(bcT[1], bc_conv[1], bc_silu)
                    tile_ready(PRO_TILES - 1)
                    for b in range(2):
                        out = nc.scalar.activation(dtT[:, b * HALF_T:(b + 1) * HALF_T], ps[0:64, b, 0:HALF_T], ACT.Copy)
                        if b:
                            out.then_inc(dt_out, 1)
            act.wait_ge(dt_out, 1)
            nc.scalar.activation(cur[0:1, 120:121], cur[0:1, 114:115], ACT.Copy).then_inc(tile_out, 1)
            store_cb(last)

            def step(s, a, i):
                if a is not None and s == 0:
                    act.wait_ge(negmax, 2 * a + 1)
                    for t in range(PCH):
                        nc.scalar.activation(probs[:, t * SEQ:(t + 1) * SEQ], probs[:, t * SEQ:(t + 1) * SEQ], ACT.Exp,
                                             bias=nmx[:, t:t + 1], accum_out=lsum[:, t:t + 1]).then_inc(probs_exp, 1)
                if i is None and s == 0:
                    pass
                if i is not None and s == 1:
                    tile_ready(tile_of(i, V))
                    tile_into(tile_of(i, V), 1, vT)
                if a is not None and s == 1:
                    act.wait_ge(negmax, 2 * a + 2)
                    for t in range(2):
                        nc.scalar.activation(probs_s[:, t * DEC_SEQ:(t + 1) * DEC_SEQ],
                                             probs_s[:, t * DEC_SEQ:(t + 1) * DEC_SEQ], ACT.Exp,
                                             bias=nmx[:, PCH + t:PCH + t + 1],
                                             accum_out=lsum[:, PCH + t:PCH + t + 1]).then_inc(probs_exp, 1)
                if a is not None and s == 2:
                    for b in range(2):
                        act.wait_ge(pt_ready, 4 * a + b + 1)
                        nc.scalar.activation(pT[:, b * SEQ:(b + 1) * SEQ], ps[:, 4 + b, :], ACT.Copy
                                             ).then_inc(pt_out_act, 1)
                if i is not None and s == 3:
                    tile_ready(tile_of(i, Q))
                    if a is not None:
                        act.wait_ge(sscores_ready, a + 1)
                    tile_into(tile_of(i, Q), 0, qT, scale=HEAD_DIM ** -0.5)
                if a is not None and s == 3:
                    act.wait_ge(pts_ready, a + 1)
                    nc.scalar.activation(pT_s, ps[:, 4, :], ACT.Copy).then_inc(pts_out, 1)
                    act.wait_ge(conved, a + 1)
                    silu(xsT, conv, xs_silu)
                if a is not None and s == 4:
                    act.wait_ge(pv_ready, 2 * a + 1)
                    nc.scalar.activation(oT[:, 0:SEQ], ps[:, 5, :], ACT.Copy).then_inc(o_out, 1)
                    act.wait_ge(pv_ready, 2 * a + 2)
                    nc.scalar.activation(oT[:, SEQ:T], ps[:, 6, 0:DEC_SEQ], ACT.Copy).then_inc(o_out, 1)
                    act.wait_ge(o_out, 2 * a + 2)
                    act.wait_ge(xs_silu, a + 1)
                    nc.scalar.activation(sqT[:, 0:T], oT, ACT.Square).then_inc(o_sq, 1)
                if i is not None and s == 5:
                    tile_ready(tile_of(i, K))
                    tile_into(tile_of(i, K), 1, kT)
                if a is not None and s == 5:
                    for half, bank in ((0, 7), (1, 4)):
                        act.wait_ge(xt_ready, 2 * a + half + 1)
                        nc.scalar.activation(x_tok[:, half * HALF_T:(half + 1) * HALF_T], ps[:, bank, 0:HALF_T],
                                             ACT.Copy).then_inc(xt_out, 1)
                    act.wait_ge(att_gated, a + 1)
                    act.dma_start(u_scr[ds(a * P, P), :], oT).then_inc(ua_stored, 16)
                if a is not None and s == 6:
                    act.wait_ge(decay_arg, a + 1)
                    nc.scalar.activation(decay, decay, ACT.Exp).then_inc(decay_exp, 1)
                if i is not None and s == 7:
                    tile_ready(tile_of(i, ZA))
                    tile_into(tile_of(i, ZA), 0, za, func=ACT.Silu)
                if a is not None and s == 8:
                    act.wait_ge(ua_stored, 16 * a + 16)
                if i is not None and s == 9:
                    tile_ready(tile_of(i, XS))
                    if a is None:
                        act.wait_ge(pads, 3)
                    tile_padded(1, xs_raw)
                if i is not None and s == 10:
                    for half, bank in ((0, 7), (1, 4)):
                        act.wait_ge(vt_ready, 2 * i + half + 1)
                        nc.scalar.activation(v_tok[:, half * HALF_T:(half + 1) * HALF_T], ps[:, bank, 0:HALF_T],
                                             ACT.Copy).then_inc(vt_out, 1)
                if a is not None and s == 10:
                    act.wait_ge(y_gated, a + 1)
                    act.dma_start(u_scr[ds((a + HEADS) * P, P), :], y).then_inc(ys_stored, 16)
                if i is not None and s == 11:
                    tile_ready(tile_of(i, ZS))
                    tile_into(tile_of(i, ZS), 0, zs, func=ACT.Silu)

            def dt_step(s):
                if s == 0:
                    act.wait_ge(row_in, 64)
                    nc.scalar.activation(a_row, a_row, ACT.Exp).then_inc(a_exp, 1)
                    act.wait_ge(dt_exp_arg, 1)
                    nc.scalar.activation(du, du, ACT.Exp).then_inc(dt_exp, 1)
                if s == 4:
                    act.wait_ge(cum_ready, 2)
                    nc.scalar.activation(loc_rows[:, 0:SEQ], ps[0:64, 5, :], ACT.Copy).then_inc(rows_read, 1)
                    nc.scalar.activation(loc_rows[:, SEQ:T], ps[0:64, 6, 0:DEC_SEQ], ACT.Copy).then_inc(rows_read, 1)
                    act.wait_ge(rows_read, 2)
                    nc.scalar.activation(er_rows, loc_rows, ACT.Exp).then_inc(rows_read, 1)
                    act.dma_start(loc_scr, loc_rows).then_inc(rows_stored, 16)
                    act.wait_ge(rows_read, 3)
                    act.dma_start(er_scr, er_rows).then_inc(rows_stored, 16)
                    act.wait_ge(cum_ready, 3)
                    nc.scalar.activation(coef[:, :], ps[:, 7, 0:PAIRS * 32], ACT.Exp).then_inc(coef_exp, 1)

            def iteration(i, a, final=False):
                for s in range(2 * TILES):
                    for m in (2 * s + 4, 2 * s + 5):
                        if not (final and m >= IT_CHUNKS):
                            split_hi(chunk_of(i, m), m % NCH, tile_of(i, m // NCH))
                    if a is None:
                        dt_step(s)
                    step(s, a, i)

            iteration(0, None)
            with act.Fori(0, HEADS - 2) as a:
                iteration(a + 1, a)
            iteration(HEADS - 1, HEADS - 2, final=True)
            for s in range(2 * TILES):
                step(s, HEADS - 1, None)

            def w2_split(u):
                act.wait_ge(w2_in[u % 2], 16 * (u // 2 + 1))
                if u >= 2:
                    act.wait_ge(part_ready, TT * (u - 1))
                nc.scalar.activation(w2_hi[u % 2], w2_raw[u % 2], ACT.Copy).then_inc(w2_hi_done, 1)

            def m_split(s, k):
                if k == 0:
                    act.wait_ge(u_in, 16 * (s + 1))
                    if s >= 2:
                        act.wait_ge(part_ready, TT * NB * (s - 1))
                    if s < 4:
                        if s:
                            act.wait_ge(ssum_ready, s)
                        nc.scalar.activation(usq, u_raw, ACT.Square).then_inc(usq_done, 1)
                kt = STEP_GROUPS[s] * GRP + k
                nc.scalar.activation(m_hi[s % 2][:, k * T:(k + 1) * T], u_raw[:, k * T:(k + 1) * T], ACT.Copy,
                                     scale=mix_cols[:, kt:kt + 1]).then_inc(m_hi_done, 1)

            for k in range(GRP):
                m_split(0, k)
            w2_split(0)
            for s in range(STEPS):
                act.wait_ge(stat_read, s + 1)
                nc.scalar.activation(r_cur[:, s % 2, :], r_cur[:, s % 2, :], ACT.Sqrt).then_inc(r_root, 1)
                for nb in range(NB):
                    u = s * NB + nb
                    if u + 1 < UNITS:
                        w2_split(u + 1)
                    if s + 1 < STEPS:
                        m_split(s + 1, nb)
            for t in range(TT):
                act.wait_ge(acc_added, TT * UNITS + t + 1)
                if t:
                    act.wait_ge(fin_sq, t)
                nc.scalar.activation(usq[:, 0:D_MODEL], acc[:, t * D_MODEL:(t + 1) * D_MODEL], ACT.Square,
                                     accum_out=fin[:, 0, t:t + 1]).then_inc(fin_sq, 1)
                act.wait_ge(fin_ms, t + 1)
                nc.scalar.activation(fin[:, 2, t:t + 1], fin[:, 1, t:t + 1], ACT.Sqrt).then_inc(fin_root, 1)

        @block.vector
        def _(dve):
            seq = [0, 0]

            def did(ins):
                ins.then_inc(dve_seq, 1)
                seq[1] += 1

            def settle():
                dve.wait_ge(dve_seq, seq[0] + seq[1])

            def copy(dst, src):
                return nc.vector.tensor_copy(dst, src)

            nc.vector.memset(table[32:33, :], 1.0).then_inc(table_ones, 1)
            did(nc.vector.memset(osq_sum[:, :], 0.0))
            dve.wait_ge(cols_ready, 1)
            copy(conv_cols[:, :], ps[:, 0, 0:120]).then_inc(cols_read, 1)
            copy(vec_cols[:, :], ps[:, 0, 128:200]).then_inc(cols_read, 1)
            for n in range(2):
                dve.wait_ge(brow_ready, n + 1)
                copy(brow[:, n * 512:(n + 1) * 512], ps[0:16, 1 + n, :]).then_inc(brow_read, 1)
            dve.wait_ge(x_squared, TT)
            nc.vector.tensor_scalar(ssq, ssq, 1.0 / D_MODEL, EPS, ALU.mult, ALU.add).then_inc(x_ms, 1)
            dve.wait_ge(x_root, 1)
            nc.vector.reciprocal(rx, rx).then_inc(x_rinv, 1)
            dve.wait_ge(x_rinv, 1)
            for t in range(TT):
                nc.vector.tensor_scalar(x_rows[t], x_rows[t], rx[:, t:t + 1], None, ALU.mult).then_inc(x_scaled, 1)

            def split_lo(n, c):
                dve.wait_ge(w_hi_done, n + 1)
                nc.vector.tensor_tensor(w_lo[:, c, :], w_raw[:, c, :], w_hi[:, c, :].bitcast(f32), ALU.subtract
                                        ).then_inc(w_lo_done, 1)

            for k in range(KT):
                dve.wait_ge(h_hi_done, k + 1)
                nc.vector.scalar_tensor_tensor(
                    h_lo[:, k * T:(k + 1) * T].rearrange("p (b t) -> p b t", b=2),
                    ps[:, 2 * (k % 4):2 * (k % 4) + 2, 0:HALF_T], pre_cols[:, k:k + 1],
                    h_hi[:, k * T:(k + 1) * T].bitcast(f32).rearrange("p (b t) -> p b t", b=2),
                    ALU.mult, ALU.subtract).then_inc(h_lo_done, 1)
                if k >= KT - NCH:
                    split_lo(k - (KT - NCH), k - (KT - NCH))
            dve.wait_ge(xt_done, KT)
            dve.wait_ge(brow_out, 16)
            for buf in (bc_raw[0], bc_raw[1], xs_raw):
                nc.vector.memset(buf[:, 0:2], 0.0)
                nc.vector.memset(buf[:, 2 + SEQ:6 + SEQ], 0.0)
                nc.vector.memset(buf[:, 6 + T:8 + T], 0.0).then_inc(pads, 1)

            def convolve(dst, src, tap, bias, done):
                W = T + 4
                did(nc.vector.tensor_scalar(dst[:, 0:W], src[:, 0:W], tap(0), bias, ALU.mult, ALU.add))
                for k in range(1, CONV_W):
                    settle()
                    ins = nc.vector.scalar_tensor_tensor(dst[:, 0:W], src[:, k:k + W], tap(k), dst[:, 0:W],
                                                         ALU.mult, ALU.add)
                    if k < CONV_W - 1:
                        did(ins)
                    else:
                        ins.then_inc(done, 1)

            def bc_conv_step(g):
                taps = conv_cols[:, :].rearrange("p (k t) -> p k t", k=CONV_W)
                for q in range(2):
                    tile = 2 * g + q
                    ct = 16 + 4 * q + g
                    did(copy(tap_cur, taps[:, :, ds(ct, 1)].rearrange("p k t -> p (k t)")))
                    did(copy(bias_cur, convb_cols[:, ds(ct, 1)]))
                    settle()
                    dve.wait_ge(tile_out, 2 * g + 2)
                    convolve(bc_conv[q], bc_raw[q], lambda k: tap_cur[:, k:k + 1], bias_cur, bc_conved)
                    dve.wait_ge(bc_conved, 2 * g + q + 1)

            def cb_out(g, sample):
                own = cb[:, PAIRS * P:].rearrange("p (d c n) -> p d c n", d=2, c=TT)
                for bank in ((4,) if sample else (4, 5, 6, 7)):
                    dve.wait_ge(pcb_ready, 5 * g + (5 if sample else bank - 3))
                    srcs = (PCH, PCH + 1) if sample else (bank - 4,)
                    for sc in srcs:
                        base = (sc - PCH) * DEC_SEQ if sample else 0
                        first = PCH if sample else 0
                        for d in range(2):
                            o = base + (sc - first) * P
                            last = nc.vector.tensor_tensor(own[:, d, sc, :], ps[:, bank, o:o + P], tri_incl[d],
                                                           ALU.mult)
                        for d, lc, sc0, n, pair0 in RUNS:
                            if sc0 <= sc < sc0 + n:
                                pr, o = pair0 + sc - sc0, base + (lc - first) * P
                                last = copy(cb[:, pr * P:(pr + 1) * P], ps[:, bank, o:o + P])
                    last.then_inc(pcb_read, 1)

            def bc_steps(g, post):
                for s in range(4):
                    for m in (2 * s + 4, 2 * s + 5):
                        split_lo(2 * NCH * g + m, m % NCH)
                    if post is not None:
                        if s == 0:
                            bc_conv_step(post)
                        if s == 2:
                            cb_out(post, False)
                        if s == 3:
                            cb_out(post, True)

            bc_steps(0, None)
            BC_SEQ = 12
            start = seq[1]
            with dve.Fori(0, SSM_GROUPS - 1) as g:
                seq[:] = [start + BC_SEQ * g, 0]
                bc_steps(g + 1, g)
                assert seq[1] == BC_SEQ, seq[1]
            seq[:] = [0, start + BC_SEQ * (SSM_GROUPS - 1)]
            last_g = SSM_GROUPS - 1
            dt_n = 2 * NCH * SSM_GROUPS
            for s in range(2):
                for m in (2 * s + 4, 2 * s + 5):
                    split_lo(dt_n + m, m % NCH)
                if s == 0:
                    bc_conv_step(last_g)
            cb_out(last_g, False)
            cb_out(last_g, True)

            def tt(out, a, b, op):
                did(nc.vector.tensor_tensor(out, a, b, op))

            def dt_step(s):
                if s == 0:
                    dve.wait_ge(row_in, 64)
                    dve.wait_ge(dtt_ready, 1)
                    per_chunk = lambda t: t.rearrange("p (c n) -> p c n", c=TT)
                    tt(per_chunk(dx), per_chunk(ps[:, 5, 0:W6]),
                       dtb_row.unsqueeze(1).broadcast_to([P, TT, 64]), ALU.add)
                    settle()
                    nc.vector.scalar_tensor_tensor(du, dx, -1.0, dx, ALU.mult, ALU.min).then_inc(dt_exp_arg, 1)
                    dve.wait_ge(dt_exp, 1)
                    did(nc.vector.tensor_scalar(dz, du, 2.0, None, ALU.add))
                    settle()
                    did(nc.vector.reciprocal(dz, dz))
                    settle()
                    tt(dz, dz, du, ALU.mult)
                    settle()
                    tt(dz2, dz, dz, ALU.mult)
                    settle()
                    did(nc.vector.tensor_scalar(dp, dz2, 1.0 / 15.0, None, ALU.mult))
                    for n in (13, 11, 9, 7, 5, 3):
                        settle()
                        did(nc.vector.scalar_tensor_tensor(dp, dp, 1.0 / n, dz2, ALU.add, ALU.mult))
                    settle()
                    did(nc.vector.scalar_tensor_tensor(dp, dp, 1.0, dz, ALU.add, ALU.mult))
                    did(nc.vector.tensor_scalar(dx, dx, 0.0, None, ALU.max))
                    settle()
                    did(nc.vector.scalar_tensor_tensor(dt_cols[:, :], dp, 2.0, dx, ALU.mult, ALU.add))
                    dve.wait_ge(a_exp, 1)
                    settle()
                    nc.vector.scalar_tensor_tensor(
                        per_chunk(adt), per_chunk(dt_cols[:, :]), -1.0,
                        a_row.unsqueeze(1).broadcast_to([P, TT, 64]), ALU.mult, ALU.mult).then_inc(adt_ready, 1)
                if s == 4:
                    dve.wait_ge(cum_ready, 1)
                    copy(loc_cols[:, :], ps[:, 4, 0:W6]).then_inc(loc_read, 1)
                    dve.wait_ge(coef_exp, 1)
                    coef3 = coef[:, :].rearrange("p (r h) -> p r h", h=32)
                    dt3 = dt_cols[:, :].rearrange("p (c n) -> p c n", c=TT)
                    for d, lc, sc0, n, pair0 in RUNS:
                        tt(coef3[:, pair0:pair0 + n, :], coef3[:, pair0:pair0 + n, :],
                           dt3[:, sc0:sc0 + n, 32 * d:32 * d + 32], ALU.mult)
                    dve.wait_ge(loc_read, 1)
                    settle()

            def step(s, a, i):
                if a is None:
                    return
                if s == 0:
                    taps = conv_cols[:, :].rearrange("p (k t) -> p k t", k=CONV_W)
                    did(copy(tap_cur, taps[:, :, ds(a, 1)].rearrange("p k t -> p (k t)")))
                    did(copy(bias_cur, convb_cols[:, ds(a, 1)]))
                    did(copy(skip_cur, skip_cols[:, ds(a, 1)]))
                    dve.wait_ge(scores_ready, PCH * a + PCH)
                    dve.wait_ge(strip_in, 16 * a + 16)
                    did(copy(coef_cur.rearrange("p (r h) -> p r h", h=2),
                             coef[:, :].rearrange("p (r h) -> p r h", h=32)[:, :, ds(a * 2, 2)]))
                    for dst, src in ((loc_cur, loc_cols), (dt_cur, dt_cols)):
                        for d in range(2):
                            did(copy(dst[:, 12 * d:12 * d + 12].rearrange("p (h c) -> p c h", h=2),
                                     src[:, :].rearrange("p (c n) -> p c n", c=TT)[:, :, ds(a * 2 + 32 * d, 2)]))
                    for t in range(PCH):
                        o = SEQ - P - t * P
                        nc.vector.tensor_tensor_reduce(
                            out=probs[:, t * SEQ:(t + 1) * SEQ], in0=ps[:, 4 + t, :], in1=strip[:, o:o + SEQ],
                            scale=1.0, scalar=-3e38, op0=ALU.add, op1=ALU.max,
                            accum_out=mx[:, t:t + 1]).then_inc(biased, 1)
                    dve.wait_ge(biased, 6 * a + 4)
                    nc.vector.tensor_scalar(nmx[:, 0:4], mx[:, 0:4], -1.0, None, ALU.mult).then_inc(negmax, 1)
                if s == 1:
                    dve.wait_ge(sscores_ready, a + 1)
                    dve.wait_ge(probs_exp, 6 * a + 4)
                    did(nc.vector.reciprocal(rinv[:, 0:4], lsum[:, 0:4]))
                    for t in range(2):
                        o = SEQ - P - t * P
                        nc.vector.tensor_tensor_reduce(
                            out=probs_s[:, t * DEC_SEQ:(t + 1) * DEC_SEQ],
                            in0=ps[:, 4, t * DEC_SEQ:(t + 1) * DEC_SEQ], in1=strip[:, o:o + DEC_SEQ],
                            scale=1.0, scalar=-3e38, op0=ALU.add, op1=ALU.max,
                            accum_out=mx[:, 4 + t:5 + t]).then_inc(biased, 1)
                    dve.wait_ge(biased, 6 * a + 6)
                    nc.vector.tensor_scalar(nmx[:, 4:6], mx[:, 4:6], -1.0, None, ALU.mult).then_inc(negmax, 1)
                    settle()
                    for t in range(PCH):
                        nc.vector.tensor_scalar(probs[:, t * SEQ:(t + 1) * SEQ], probs[:, t * SEQ:(t + 1) * SEQ],
                                                rinv[:, t:t + 1], None, ALU.mult).then_inc(normed, 1)
                if s == 2:
                    dve.wait_ge(probs_exp, 6 * a + 6)
                    did(nc.vector.reciprocal(rinv[:, 4:6], lsum[:, 4:6]))
                    settle()
                    for t in range(2):
                        nc.vector.tensor_scalar(probs_s[:, t * DEC_SEQ:(t + 1) * DEC_SEQ],
                                                probs_s[:, t * DEC_SEQ:(t + 1) * DEC_SEQ],
                                                rinv[:, 4 + t:5 + t], None, ALU.mult).then_inc(normed, 1)
                    for b in (2, 3):
                        dve.wait_ge(pt_ready, 4 * a + b + 1)
                        copy(pT[:, b * SEQ:(b + 1) * SEQ], ps[:, 4 + b, :]).then_inc(pt_out_dve, 1)
                    dve.wait_ge(tile_out, PRO_TILES + TILES * a + XS + 1)
                    convolve(conv, xs_raw, lambda k: tap_cur[:, k:k + 1], bias_cur, conved)
                if s == 4:
                    dve.wait_ge(o_sq, a + 1)
                    tt(osq_sum[:, :], osq_sum[:, :], sqT[:, 0:T], ALU.add)
                    settle()
                    nc.vector.tensor_tensor(oT, oT, za, ALU.mult).then_inc(att_gated, 1)
                if s == 5:
                    dve.wait_ge(xt_out, 2 * a + 2)
                    dve.wait_ge(pv_ready, 2 * a + 1)
                    cc = coef_cur.rearrange("p (r h) -> p r h", h=2)
                    for n_run, (d, lc, sc0, n, pair0) in enumerate(RUNS):
                        ins = nc.vector.tensor_tensor(
                            xsc[:, pair0 * P:(pair0 + n) * P].rearrange("p (r n) -> p r n", n=64),
                            x_tok[:, sc0 * P:(sc0 + n) * P].rearrange("p (r n) -> p r n", n=64),
                            coef_cur[:, 2 * pair0:2 * (pair0 + n)].unsqueeze(2).broadcast_to([P, 2 * n, 64]),
                            ALU.mult)
                    ins.then_inc(xsc_done, 1)
                    dve.wait_ge(decay_in, 16 * a + 16)
                    dv = decay.rearrange("p (r n) -> p r n", n=P)
                    tt(dv, dv, loc_cur.unsqueeze(2).broadcast_to([P, 24, P]), ALU.subtract)
                    settle()
                    nc.vector.tensor_scalar(decay, decay, 0.0, None, ALU.min).then_inc(decay_arg, 1)
                if s == 6:
                    dve.wait_ge(decay_exp, a + 1)
                    dv = decay.rearrange("p (r n) -> p r n", n=P)
                    tt(dv, dv, dt_cur.unsqueeze(2).broadcast_to([P, 24, P]), ALU.mult)
                    settle()
                    dve.wait_ge(cb_in, 16 * a + 16)
                    for d in range(2):
                        part = decay[:, 2 * T * d:2 * T * (d + 1)].rearrange("p (h n) -> p h n", h=2)
                        own = cb[:, PAIRS * P + T * d:PAIRS * P + T * (d + 1)]
                        tt(part, part, own.unsqueeze(1).broadcast_to([P, 2, T]), ALU.mult)
                    settle()
                    nc.vector.tensor_tensor(decay[:, 0:2 * T], decay[:, 0:2 * T], decay[:, 2 * T:4 * T], ALU.add
                                            ).then_inc(wmat_done, 1)
                if s == 7:
                    dve.wait_ge(xs_silu, a + 1)
                    did(nc.vector.tensor_scalar(y, xsT, skip_cur, None, ALU.mult))
                    dve.wait_ge(er_in, 32 * a + 32)
                    for d, bp, bs, p0, p1, q0 in ((0, 5, 6, P, SEQ, P), (1, 7, 4, 0, SEQ - P, 0)):
                        dve.wait_ge(off_ready, 2 * a + d + 1)
                        tt(ytmp[:, p0:p1], ps[:, bp, p0:p1], er[:, d * T + p0:d * T + p1], ALU.mult)
                        nc.vector.tensor_tensor(ytmp[:, SEQ + q0:SEQ + q0 + P], ps[:, bs, q0:q0 + P],
                                                er[:, d * T + SEQ + q0:d * T + SEQ + q0 + P], ALU.mult
                                                ).then_inc(off_read, 1)
                        settle()
                        tt(y[:, p0:p1], y[:, p0:p1], ytmp[:, p0:p1], ALU.add)
                        dve.wait_ge(off_read, 2 * a + d + 1)
                        tt(y[:, SEQ + q0:SEQ + q0 + P], y[:, SEQ + q0:SEQ + q0 + P],
                           ytmp[:, SEQ + q0:SEQ + q0 + P], ALU.add)
                        settle()
                if s == 9:
                    dve.wait_ge(diag_ready, 2 * a + 1)
                    tt(y[:, 0:SEQ], y[:, 0:SEQ], ps[:, 5, :], ALU.add)
                    dve.wait_ge(diag_ready, 2 * a + 2)
                    tt(y[:, SEQ:T], y[:, SEQ:T], ps[:, 6, 0:DEC_SEQ], ALU.add)
                    settle()
                    dve.wait_ge(tile_out, PRO_TILES + TILES * a + ZS + 1)
                    nc.vector.tensor_tensor(y, y, zs, ALU.mult).then_inc(y_gated, 1)
                if s == 11:
                    dve.wait_ge(ys_stored, 16 * a + 16)

            def iteration(i, a, final=False):
                for s in range(2 * TILES):
                    for m in (2 * s + 4, 2 * s + 5):
                        if not (final and m >= IT_CHUNKS):
                            split_lo(chunk_of(i, m), m % NCH)
                    if a is None:
                        dt_step(s)
                    step(s, a, i)

            iteration(0, None)
            start = seq[1]
            with dve.Fori(0, HEADS - 2) as a:
                seq[:] = [start + DVE_PER_PASS * a, 0]
                iteration(a + 1, a)
                assert seq[1] == DVE_PER_PASS, seq[1]
            seq[:] = [0, start + DVE_PER_PASS * (HEADS - 2)]
            iteration(HEADS - 1, HEADS - 2, final=True)
            for s in range(2 * TILES):
                step(s, HEADS - 1, None)

            dve.wait_ge(ua_stored, 16 * HEADS)
            dve.wait_ge(ys_stored, 16 * SSM_TILES)
            for t in range(TT):
                nc.vector.memset(acc[:, t * D_MODEL:(t + 1) * D_MODEL], 0.0).then_inc(acc_added, 1)

            def w2_split(u):
                dve.wait_ge(w2_hi_done, u + 1)
                nc.vector.tensor_tensor(w2_lo[u % 2], w2_raw[u % 2], w2_hi[u % 2].bitcast(f32), ALU.subtract
                                        ).then_inc(w2_lo_done, 1)

            def m_split(s, k):
                if k == 0:
                    if s:
                        dve.wait_ge(stat_ready, s)
                    if s < 4:
                        dve.wait_ge(usq_done, s + 1)
                        nc.vector.tensor_reduce(ssum, usq.rearrange("p (k t) -> p t k", k=GRP),
                                                AX.X, ALU.add).then_inc(ssum_ready, 1)
                    else:
                        copy(ssum, osq_sum[:, :]).then_inc(ssum_ready, 1)
                dve.wait_ge(m_hi_done, GRP * s + k + 1)
                kt = STEP_GROUPS[s] * GRP + k
                nc.vector.scalar_tensor_tensor(
                    m_lo[s % 2][:, k * T:(k + 1) * T], u_raw[:, k * T:(k + 1) * T], mix_cols[:, kt:kt + 1],
                    m_hi[s % 2][:, k * T:(k + 1) * T].bitcast(f32), ALU.mult, ALU.subtract).then_inc(m_lo_done, 1)

            for k in range(GRP):
                m_split(0, k)
            w2_split(0)
            for s in range(STEPS):
                dve.wait_ge(stat_ready, s + 1)
                nc.vector.tensor_scalar(r_cur[:, s % 2, :], ps[:, 6, 0:TT],
                                        1.0 / (GRP * P if s < 4 else D_MODEL), EPS, ALU.mult, ALU.add
                                        ).then_inc(stat_read, 1)
                dve.wait_ge(r_root, s + 1)
                nc.vector.reciprocal(r_cur[:, s % 2, :], r_cur[:, s % 2, :]).then_inc(r_ready, 1)
                dve.wait_ge(r_ready, s + 1)
                for nb in range(NB):
                    u = s * NB + nb
                    if u + 1 < UNITS:
                        w2_split(u + 1)
                    if s + 1 < STEPS:
                        m_split(s + 1, nb)
                    for t in range(TT):
                        dve.wait_ge(part_ready, u * TT + t + 1)
                        dve.wait_ge(acc_added, 6 * (s * NB) + t + 1)
                        o = t * D_MODEL + nb * NBW
                        nc.vector.scalar_tensor_tensor(acc[:, o:o + NBW], ps[:, t, :], r_cur[:, s % 2, t:t + 1],
                                                       acc[:, o:o + NBW], ALU.mult, ALU.add).then_inc(acc_added, 1)
            dve.wait_ge(g_in, 16)
            for t in range(TT):
                row = acc[:, t * D_MODEL:(t + 1) * D_MODEL]
                dve.wait_ge(fin_sq, t + 1)
                nc.vector.tensor_scalar(fin[:, 1, t:t + 1], fin[:, 0, t:t + 1], 1.0 / D_MODEL, EPS, ALU.mult, ALU.add
                                        ).then_inc(fin_ms, 1)
                did(nc.vector.tensor_tensor(row, row, g_row, ALU.mult))
                dve.wait_ge(fin_root, t + 1)
                did(nc.vector.reciprocal(fin[:, 0, t:t + 1], fin[:, 2, t:t + 1]))
                settle()
                dve.wait_ge(xb_in[t % 3], 16 * (t // 3 + 1))
                nc.vector.scalar_tensor_tensor(row, row, fin[:, 0, t:t + 1], x_back[t % 3], ALU.mult, ALU.add
                                               ).then_inc(fin_done, 1)


_INS = ["x_prompt", "x_sample", "pre_norm_g", "w_in", "rel_bias_table", "attn_norm_g", "conv_w", "conv_b",
        "dt_bias_fwd", "dt_bias_bwd", "a_log_fwd", "a_log_bwd", "d_skip", "ssm_norm_g", "w_out", "post_norm_g"]
_SCRATCH = [("u_scr", (2 * 16 * 128, 768)), ("brow_scr", (16, 1024)), ("strip_scr", (16 * 128, 896)),
            ("loc_scr", (64, 768)), ("er_scr", (64, 768)), ("cb_scr", (4 * 128, PAIRS * 128 + 2 * 768))]


def kernel(**inputs):
    import concourse.bacc as bacc
    from concourse.bass_utils import run_bass_kernel_spmd

    nc = bacc.Bacc("TRN2", target_bir_lowering=False, num_devices=1, dynamic_dma_scratch_size=1024)
    f32 = mybir.dt.float32
    arrays, args = {}, []
    squares, hots = shape_constants()
    for name, a in [(n, inputs[n]) for n in _INS] + [("squares", squares), ("hots", hots)]:
        a = np.ascontiguousarray(a)
        arrays[f"in_{name}"] = a
        args.append(nc.dram_tensor(f"in_{name}", a.shape, f32, kind="ExternalInput").ap())
    for name, shape in _SCRATCH:
        args.append(nc.dram_tensor(name, shape, f32).ap())
    for name, shape in (("y_prompt", (1, SEQ, D_MODEL)), ("y_sample", (1, DEC_SEQ, D_MODEL))):
        args.append(nc.dram_tensor(name, shape, f32, kind="ExternalOutput").ap())
    encoder(nc, *args)
    r = run_bass_kernel_spmd(nc, [arrays], core_ids=[0])
    return r.results[0]["y_prompt"], r.results[0]["y_sample"]
```

```python
import math
from contextlib import ExitStack

import numpy as np

import concourse.bass as bass
from concourse import mybir

P = 128
D_MODEL = 2048
SEQ, DEC_SEQ = 512, 256
T = SEQ + DEC_SEQ
HEADS, HEAD_DIM = 16, 128
WINDOWS = ((128, 1), (512, 4), (2048, 16))
N_BUCKETS, BUCKET_MAX_DIST = 32, 1024
SSM_HEADS, SSM_GROUPS = 32, 4
Q_SCALE = HEAD_DIM ** -0.5
CONV_W = 5
EPS = 1e-6
NEG = -1e30

KT = D_MODEL // P
TT = T // P
PCH = SEQ // P
HALF_T = T // 2
KC = 4
NCH = KT // KC
SSM_TILES = 16
COL_Q, COL_K, COL_V, COL_ZA, COL_ZS, COL_XS, COL_B, COL_C, COL_DT = (
    0, 2048, 4096, 6144, 8192, 10240, 12288, 12800, 13312)
LOOP_COLS = (COL_V, COL_Q, COL_K, COL_ZA, COL_XS, COL_ZS)
V, Q, K, ZA, XS, ZS = range(6)
TILES = len(LOOP_COLS)
PRO_TILES = 2 * SSM_GROUPS + 1
PRO_CHUNKS = PRO_TILES * NCH
IT_CHUNKS = TILES * NCH
STAGE = 20112
STRIP = SEQ + 3 * P
BROW = 1024

RUNS = []
for _d in range(2):
    for _first, _last in ((0, PCH), (PCH, TT)):
        for _lc in range(_first, _last):
            _src = range(_first, _lc) if _d == 0 else range(_lc + 1, _last)
            if len(_src):
                RUNS.append((_d, _lc, _src[0], len(_src), sum(r[3] for r in RUNS)))
PAIRS = sum(r[3] for r in RUNS)

GRP = 4
STEPS = 32 // GRP
STEP_GROUPS = (4, 5, 6, 7, 0, 1, 2, 3)
NB = 4
NBW = D_MODEL // NB
UNITS = STEPS * NB
LAST_ORDER = [(0, t) for t in range(TT)] + [(nb, t) for t in range(TT) for nb in range(1, NB)]

X_TURNS = {8: 4, 12: 5}
W_TURNS = {24: (0,), 27: (1,), 31: (2, 3)}

DVE_PER_PASS = 28


def t5_bucket(rel):
    nb = N_BUCKETS // 2
    exact = nb // 2
    n = np.abs(rel)
    nf = np.maximum(n, 1).astype(np.float32)
    large = exact + (np.log(nf / np.float32(exact)) / np.float32(math.log(BUCKET_MAX_DIST / exact))
                     * np.float32(nb - exact)).astype(np.int32)
    return np.where(rel > 0, nb, 0) + np.where(n < exact, n, np.minimum(large, nb - 1))


def shape_constants():
    k, s = np.arange(P)[:, None], np.arange(P)[None]
    sq = np.concatenate([k == s, k <= s, k >= s, k > s, k < s, np.ones((P, P))], 1).astype(np.float32)
    rel = np.arange(BROW) - (SEQ - 1)
    count = sum(((rel % dil == 0) & (np.abs(rel) <= win // 2)).astype(np.int64) for win, dil in WINDOWS)
    hot = np.zeros((N_BUCKETS + 1, BROW), np.float32)
    hot[t5_bucket(rel), np.arange(BROW)] = 1.0
    hot[N_BUCKETS] = np.where(count > 0, np.log(np.maximum(count, 1)), NEG)
    return sq, hot


def encoder(nc, x_prompt, x_sample, pre_g, w_in, rel_table, attn_g, conv_w, conv_b, dtb_f, dtb_b,
            alog_f, alog_b, d_skip, ssm_g, w_out, post_g, squares, hots,
            u_scr, brow_scr, strip_scr, loc_scr, er_scr, cb_scr, y_prompt, y_sample):
    f32, f32r = mybir.dt.float32, mybir.dt.float32r
    ALU, ACT, AX = mybir.AluOpType, mybir.ActivationFunctionType, mybir.AxisListType
    ds = bass.ds

    ctx = ExitStack()
    with ctx:
        def sb(name, shape, dt=f32):
            return ctx.enter_context(nc.sbuf_tensor(name, shape, dt))

        def sem(name):
            return ctx.enter_context(nc.semaphore(name))

        h_hi = sb("h_hi", [P, KT * T], f32r)
        h_lo = sb("h_lo", [P, KT * T], f32r)
        w_raw = sb("w_raw", [P, NCH, KC * P])
        w_hi = sb("w_hi", [P, NCH, KC * P], f32r)
        w_lo = sb("w_lo", [P, NCH, KC * P], f32r)
        q_hi, q_lo, k_hi, k_lo = (sb(n, [P, T], f32r) for n in ("q_hi", "q_lo", "k_hi", "k_lo"))
        sq_c = sb("sq_c", [P, 6 * P])
        ident, tri_f, tri_b, stri_f, stri_b, ones = (sq_c[:, i * P:(i + 1) * P] for i in range(6))
        tri_incl, tri_strict = (tri_f, tri_b), (stri_f, stri_b)
        conv_cols = sb("conv_cols", [P, CONV_W * 24])
        vec_cols = sb("vec_cols", [P, 72])
        convb_cols, pre_cols, mix_cols = vec_cols[:, 0:24], vec_cols[:, 24:40], vec_cols[:, 40:72]
        skip_cols = sb("skip_cols", [P, SSM_TILES])
        loc_dt = sb("loc_dt", [P, 2 * TT * 64])
        loc_cols, dt_cols = loc_dt[:, 0:TT * 64], loc_dt[:, TT * 64:]
        coef = sb("coef", [P, PAIRS * 32])
        osq_sum = sb("osq_sum", [P, T])
        cur = sb("cur", [P, 128])
        tap_cur, bias_cur, skip_cur = cur[:, 0:5], cur[:, 5:6], cur[:, 6:7]
        coef_cur, loc_cur, dt_cur = cur[:, 8:36], cur[:, 36:60], cur[:, 60:84]
        mx, nmx, lsum, rinv = (cur[:, 84 + 6 * i:90 + 6 * i] for i in range(4))
        ssq, rx = cur[:, 108:114], cur[:, 114:120]
        stage = sb("stage", [P, STAGE])
        at = [0]

        def carve(n):
            at[0] += n
            assert at[0] <= STAGE
            return stage[:, at[0] - n:at[0]]

        XW = T + 8
        xs_raw = carve(XW)
        vT, v_tok, za, xsT, zs = (carve(T) for _ in range(5))
        strip = carve(STRIP)
        probs = carve(4 * SEQ)
        probs_s = carve(2 * DEC_SEQ)
        pT = carve(4 * SEQ)
        pT_s = carve(2 * DEC_SEQ)
        sqT = carve(XW)
        decay = carve(4 * T)
        er = carve(2 * T)
        cb = carve(PAIRS * P + 2 * T)
        x_tok = carve(T)
        conv = sqT
        xsc = pT[:, 0:PAIRS * P]
        y, ytmp = probs[:, 0:T], probs[:, T:2 * T]
        probs_at = XW + 5 * T + STRIP
        oT = stage[:, probs_at + 2 * T:probs_at + 3 * T]
        x_rows = [stage[:, t * D_MODEL:(t + 1) * D_MODEL] for t in range(TT)]
        x_junk = stage[:, TT * D_MODEL:(TT + 1) * D_MODEL]
        s0 = (TT + 1) * D_MODEL
        par_a, par_b = stage[0:120, s0:s0 + P], stage[0:72, s0 + P:s0 + 2 * P]
        table = stage[0:33, s0 + 2 * P:s0 + 2 * P + 16]
        hot = stage[0:33, s0 + 512:s0 + 512 + BROW]
        brow = stage[0:16, s0 + 2048:s0 + 2048 + BROW]
        bc_raw = [decay[:, 0:XW], decay[:, XW:2 * XW]]
        bc_conv = [decay[:, 2 * XW:3 * XW], er[:, 0:XW]]
        bcT = [probs[:, 0:T], probs[:, T:2 * T]]
        dtT = pT[0:64, 0:T]
        W6 = TT * 64
        dx, du, dz, dz2, dp = (pT[:, T:T + W6], pT[:, T + W6:T + 2 * W6], pT[:, T + 2 * W6:T + 3 * W6],
                               probs_s[:, 0:W6], pT_s[:, 0:W6])
        dtb_row, a_row = sqT[:, 0:64], sqT[:, 64:128]
        loc_rows = x_tok[0:64, :]
        er_rows = xsT[0:64, 0:T]
        adt = sqT[:, 128:128 + W6]

        MG = GRP * T
        m_hi = [h_hi[:, i * MG:(i + 1) * MG] for i in range(2)]
        m_lo = [h_lo[:, i * MG:(i + 1) * MG] for i in range(2)]
        WG = GRP * NBW
        w2_hi = [h_hi[:, 2 * MG + i * WG:2 * MG + (i + 1) * WG] for i in range(2)]
        w2_lo = [h_lo[:, 2 * MG + i * WG:2 * MG + (i + 1) * WG] for i in range(2)]
        w2_hi += [h_hi[:, 2 * MG + 2 * WG:2 * MG + 3 * WG], h_hi[:, 0:WG]]
        w2_lo += [h_lo[:, 2 * MG + 2 * WG:2 * MG + 3 * WG], h_lo[:, 0:WG]]
        w2_slot = lambda u: u % 2 if u < UNITS - 2 else u - (UNITS - 4)
        acc = stage[:, 0:TT * D_MODEL]
        w2_raw = [stage[:, TT * D_MODEL + i * WG:TT * D_MODEL + (i + 1) * WG] for i in range(2)]
        u_raw = stage[:, TT * D_MODEL + 2 * WG:TT * D_MODEL + 2 * WG + MG]
        w2_first = w_raw[:, :, :].rearrange("p a b -> p (a b)")
        u_first = [vT, w2_first[:, 0:T], w2_first[:, T:2 * T], strip[:, 0:T]]
        usq = w2_first[:, 0:T]
        usq_first = xs_raw[:, 0:T]
        ssum = loc_dt[:, :]
        g_row = w_raw[:, :, :].rearrange("p a b -> p (a b)")
        x_back = [stage[:, TT * D_MODEL + i * D_MODEL:TT * D_MODEL + (i + 1) * D_MODEL] for i in (2, 0, 1)]
        XB = len(x_back)
        fin_junk = loc_dt[:, 0:NBW]
        r_cur = coef[:, 0:2 * TT].rearrange("p (a t) -> p a t", a=2)
        fin = coef[:, 2 * TT:(NB + 5) * TT].rearrange("p (a t) -> p a t", t=TT)
        fin_parts, fin_sum, fin_mean, fin_rms = fin[:, 0:NB, :], fin[:, NB, :], fin[:, NB + 1, :], fin[:, NB + 2, :]

        ps = ctx.enter_context(nc.psum_tensor("ps", [P, 8, 512], f32))

        x_in = [sem(f"x_in{t}") for t in range(TT)]
        skip_in = sem("skip_in")
        small_in, hot_in, brow_out = sem("small_in"), sem("hot_in"), sem("brow_out")
        strip_out = [sem(f"strip_out{i}") for i in range(2)]
        row_in = sem("row_in")
        x_squared, x_ms, x_root, x_rinv, x_scaled = (sem(n) for n in (
            "x_squared", "x_ms", "x_root", "x_rinv", "x_scaled"))
        cols_ready, cols_read, brow_ready, brow_read = (sem(n) for n in (
            "cols_ready", "cols_read", "brow_ready", "brow_read"))
        table_ones = sem("table_ones")
        xt_done, h_hi_done, h_lo_done = sem("xt_done"), sem("h_hi_done"), sem("h_lo_done")
        w_in_s = [sem(f"w_in{c}") for c in range(NCH)]
        w_hi_done, w_lo_done, w_used = sem("w_hi_done"), sem("w_lo_done"), sem("w_used")
        qk_hi_done = sem("qk_hi_done")
        tile_done, tile_out = sem("tile_done"), sem("tile_out")
        pads = sem("pads")
        bc_conved, bc_silu, pcb_ready, pcb_read, cb_stored = (sem(n) for n in (
            "bc_conved", "bc_silu", "pcb_ready", "pcb_read", "cb_stored"))
        dt_out, dtt_ready, dt_exp_arg, dt_exp, a_exp, adt_ready = (sem(n) for n in (
            "dt_out", "dtt_ready", "dt_exp_arg", "dt_exp", "a_exp", "adt_ready"))
        cum_ready, loc_read, rows_read, coef_exp, coef_done = (sem(n) for n in (
            "cum_ready", "loc_read", "rows_read", "coef_exp", "coef_done"))
        rows_stored = sem("rows_stored")
        strip_in, decay_in, er_in, cb_in = sem("strip_in"), sem("decay_in"), sem("er_in"), sem("cb_in")
        scores_ready, sscores_ready, pt_ready, pts_ready, pv_ready, vt_ready = (sem(n) for n in (
            "scores_ready", "sscores_ready", "pt_ready", "pts_ready", "pv_ready", "vt_ready"))
        biased, negmax, probs_exp, normed, pt_out_act, pt_out_dve, pts_out = (sem(n) for n in (
            "biased", "negmax", "probs_exp", "normed", "pt_out_act", "pt_out_dve", "pts_out"))
        o_out, o_sq, att_gated, ua_stored, vt_out = (sem(n) for n in (
            "o_out", "o_sq", "att_gated", "ua_stored", "vt_out"))
        conved, xs_silu, xt_ready, xt_out, xsc_done, decay_arg, decay_exp, wmat_done = (sem(n) for n in (
            "conved", "xs_silu", "xt_ready", "xt_out", "xsc_done", "decay_arg", "decay_exp", "wmat_done"))
        off_ready, off_read, diag_ready, y_gated, ys_stored = (sem(n) for n in (
            "off_ready", "off_read", "diag_ready", "y_gated", "ys_stored"))
        dve_seq = sem("dve_seq")
        u_first_in = [sem(f"u_first_in{k}") for k in range(GRP)]
        u_in, w2_in = sem("u_in"), [sem(f"w2_in{i}") for i in range(2)]
        g_in = sem("g_in")
        usq_added = sem("usq_added")
        usq_done, m_hi_done, m_lo_done, w2_hi_done, w2_lo_done = (sem(n) for n in (
            "usq_done", "m_hi_done", "m_lo_done", "w2_hi_done", "w2_lo_done"))
        ssum_ready, stat_ready, stat_read, r_root, r_ready, part_ready, acc_added = (sem(n) for n in (
            "ssum_ready", "stat_ready", "stat_read", "r_root", "r_ready", "part_ready", "acc_added"))
        xb_in = [sem(f"xb_in{i}") for i in range(XB)]
        fin_sq, fin_ms, fin_root, fin_done, y_out = (sem(n) for n in (
            "fin_sq", "fin_ms", "fin_root", "fin_done", "y_out"))

        w_rows = w_in[0].rearrange("(k p) n -> p k n", p=P)
        w2_rows = w_out[0].rearrange("(k p) n -> p k n", p=P)
        chunk_of = lambda i, m: PRO_CHUNKS + IT_CHUNKS * i + m
        tile_of = lambda i, j: PRO_TILES + TILES * i + j
        block = ctx.enter_context(nc.Block())

        @block.sync
        def _(sp):
            def load_x(t):
                src = x_prompt[0, t * P:(t + 1) * P, :] if t < PCH else x_sample[0, (t - PCH) * P:(t - PCH + 1) * P, :]
                sp.dma_start(x_rows[t], src).then_inc(x_in[t], 16)

            load_x(0)
            sp.dma_start(sq_c[:, :], squares).then_inc(small_in, 16)
            sp.dma_start(par_a, conv_w[0].rearrange("k (t p) -> (k t) p", p=P)).then_inc(small_in, 16)
            r = 0
            for v in (conv_b, pre_g, attn_g, ssm_g):
                n = v.shape[1] // P
                sp.dma_start(par_b[r:r + n, :], v[0].rearrange("(t p) -> t p", p=P)).then_inc(small_in, 16)
                r += n
            for t in range(1, TT):
                load_x(t)

            def load_w(n, col, c, width=P, waited=False):
                src = w_rows[:, c * KC:(c + 1) * KC, ds(col, width)]
                if not waited and (not isinstance(n, int) or n >= NCH):
                    sp.wait_ge(w_lo_done, n - NCH + 1)
                sp.dma_start(w_raw[:, c, :].rearrange("p (k n) -> p k n", k=KC)[:, :, 0:width], src
                             ).then_inc(w_in_s[c], 16)

            for c in range(NCH):
                load_w(c, COL_B, c)
            sp.dma_start(table[0:32, :], rel_table).then_inc(hot_in, 16)
            sp.dma_start(hot, hots).then_inc(hot_in, 16)
            for c in range(NCH):
                load_w(NCH + c, COL_C, c)
            for c in range(2):
                load_w(2 * NCH + c, COL_B + P, c)
            sp.wait_ge(brow_read, 2)
            sp.dma_start(brow_scr, brow).then_inc(brow_out, 16)

            def make_strips(h, done):
                sp.dma_start(strip_scr[h * P:(h + 2) * P, :],
                             bass.AP(brow_scr.tensor, h * BROW + P - 1, [[BROW, 2], [-1, P], [1, STRIP]])
                             ).then_inc(done, 16)

            for c in range(2, NCH):
                load_w(2 * NCH + c, COL_B + P, c)
            sp.wait_ge(brow_out, 16)
            make_strips(0, strip_out[0])
            sp.wait_ge(xt_done, 2 * KT)
            for q, v in enumerate((dtb_f, dtb_b)):
                sp.dma_start(dtb_row[:, 32 * q:32 * q + 32], v.partition_broadcast(P).rearrange("p a b -> p (a b)")
                             ).then_inc(row_in, 16)
            for q, v in enumerate((alog_f, alog_b)):
                sp.dma_start(a_row[:, 32 * q:32 * q + 32], v.partition_broadcast(P).rearrange("p a b -> p (a b)")
                             ).then_inc(row_in, 16)
            for c in range(NCH):
                load_w(3 * NCH + c, COL_C + P, c)
            with sp.Fori(2, SSM_GROUPS) as g:
                gcol = sp.snap(g * P)
                for j, base in enumerate((COL_B, COL_C)):
                    for c in range(NCH):
                        load_w(2 * NCH * g + NCH * j + c, gcol + base, c)
            for c in range(NCH):
                load_w(2 * NCH * SSM_GROUPS + c, COL_DT, c, width=64)

            def reload(a):
                sp.dma_start(decay.rearrange("p (d n) -> p d n", d=2),
                             loc_scr.rearrange("(d h) t -> d (h t)", d=2)[:, ds(a * 2 * T, 2 * T)]
                             .partition_broadcast(P)).then_inc(decay_in, 16)
                for h in range(2):
                    sp.dma_start(er[64 * h:64 * h + 64, :].rearrange("p (d n) -> p d n", d=2),
                                 er_scr.rearrange("(d h) t -> d (h t)", d=2)[:, ds(a * 2 * T + h * T, T)]
                                 .partition_broadcast(64)).then_inc(er_in, 16)
                sp.dma_start(cb, cb_scr[ds((a // 4) * P, P), :]).then_inc(cb_in, 16)

            def load_strip(i):
                if not isinstance(i, int):
                    sp.wait_ge(biased, 6 * i)
                sp.dma_start(strip, strip_scr[ds(i * P, P), :]).then_inc(strip_in, 16)

            def iteration(i, a):
                for m in range(IT_CHUNKS):
                    j, c = divmod(m, NCH)
                    if m == NCH and a is not None:
                        sp.wait_ge(w_lo_done, chunk_of(i, m) - NCH + 1)
                        reload(a)
                        load_w(chunk_of(i, m), i * P + LOOP_COLS[j], c, waited=True)
                    else:
                        load_w(chunk_of(i, m), i * P + LOOP_COLS[j], c)
                    if m == 15:
                        load_strip(i)

            for m in range(IT_CHUNKS):
                j, c = divmod(m, NCH)
                load_w(chunk_of(0, m), LOOP_COLS[j], c)
                if m % 2 and m + 1 < HEADS:
                    make_strips(m + 1, strip_out[1])
            sp.wait_ge(strip_out[0], 16)
            load_strip(0)
            sp.wait_ge(strip_out[1], 16 * (HEADS // 2 - 1))
            sp.wait_ge(rows_stored, 32)
            sp.wait_ge(cb_stored, 16 * SSM_GROUPS)
            with sp.Fori(0, HEADS - 1) as a:
                iteration(a + 1, a)
            sp.wait_ge(y_gated, HEADS - 1)
            reload(HEADS - 1)

            sp.wait_ge(w_lo_done, PRO_CHUNKS + IT_CHUNKS * HEADS)
            sp.dma_start(w2_first.rearrange("p (k n) -> p k n", k=GRP),
                         w2_rows[:, STEP_GROUPS[0] * GRP:(STEP_GROUPS[0] + 1) * GRP, 0:NBW]).then_inc(w2_in[0], 16)
            sp.wait_ge(ys_stored, 16 * (SSM_TILES - 1))
            for k in range(GRP):
                if k == 0:
                    sp.wait_ge(vt_ready, 2 * HEADS)
                if k == 1:
                    sp.wait_ge(w2_lo_done, 1)
                if k == 3:
                    sp.wait_ge(biased, 6 * HEADS)
                row = (STEP_GROUPS[0] * GRP + k) * P
                sp.dma_start(u_first[k], u_scr[row:row + P, :]).then_inc(u_first_in[k], 16)
            sp.wait_ge(m_lo_done, 3)
            sp.wait_ge(usq_done, 2)
            sp.dma_start(w2_first.rearrange("p (k n) -> p k n", k=GRP),
                         w2_rows[:, STEP_GROUPS[0] * GRP:(STEP_GROUPS[0] + 1) * GRP, NBW:2 * NBW]
                         ).then_inc(w2_in[1], 16)

            sp.wait_ge(ua_stored, 16 * HEADS)
            sp.wait_ge(ys_stored, 16 * SSM_TILES)
            sp.wait_ge(m_lo_done, GRP)
            sp.wait_ge(w2_lo_done, 2)

            def load_u(s):
                if s > 1:
                    sp.wait_ge(m_lo_done, GRP * s)
                    sp.wait_ge(ssum_ready, s)
                g0 = STEP_GROUPS[s] * GRP
                sp.dma_start(u_raw.rearrange("p (k t) -> p k t", k=GRP),
                             u_scr[g0 * P:(g0 + GRP) * P, :].rearrange("(k p) t -> p k t", p=P)).then_inc(u_in, 16)

            def load_w2(u):
                if u >= 2:
                    sp.wait_ge(w2_lo_done, u - 1)
                s, nb = divmod(u, NB)
                k0 = STEP_GROUPS[s] * GRP
                sp.dma_start(w2_raw[u % 2].rearrange("p (k n) -> p k n", k=GRP),
                             w2_rows[:, k0:k0 + GRP, nb * NBW:(nb + 1) * NBW]).then_inc(w2_in[u % 2], 16)

            load_w2(2)
            load_w2(3)
            load_u(1)
            for u in range(4, UNITS):
                load_w2(u)
                if u > NB and u % NB == 2 and u // NB + 1 < STEPS:
                    load_u(u // NB + 1)
                if u == 5 * NB:
                    sp.wait_ge(ssum_ready, 5)
                    sp.dma_start(g_row, post_g.partition_broadcast(P).rearrange("p a b -> p (a b)")
                                 ).then_inc(g_in, 16)
            def x_src(t):
                return x_prompt[0, t * P:(t + 1) * P, :] if t < PCH else x_sample[0, (t - PCH) * P:(t - PCH + 1) * P, :]
            sp.wait_ge(m_lo_done, GRP * STEPS)
            for t in range(XB):
                if t >= 1:
                    sp.wait_ge(w2_lo_done, UNITS - XB + 1 + t)
                sp.dma_start(x_back[t], x_src(t)).then_inc(xb_in[t], 16)
            for t in range(TT):
                dst = y_prompt[0, t * P:(t + 1) * P, :] if t < PCH else y_sample[0, (t - PCH) * P:(t - PCH + 1) * P, :]
                for h in range(2):
                    c0, c1 = h * D_MODEL // 2, (h + 1) * D_MODEL // 2
                    sp.wait_ge(fin_done, 2 * t + h + 1)
                    sp.dma_start(dst[:, c0:c1], acc[:, t * D_MODEL + c0:t * D_MODEL + c1]).then_inc(y_out, 16)
                if t + XB < TT:
                    sp.dma_start(x_back[t], x_src(t + XB)).then_inc(xb_in[t], 16)
            sp.wait_ge(y_out, 2 * 16 * TT)

        @block.tensor
        def _(pe):
            pe.wait_ge(small_in, 16 * 6)
            nc.tensor.transpose(ps[:, 7, 0:120], par_a, ident[0:120, 0:120])
            nc.tensor.transpose(ps[:, 7, 128:200], par_b, ident[0:72, 0:72]).then_inc(cols_ready, 1)
            pe.wait_ge(cols_read, 2)
            for half in range(2):
                for k in range(KT):
                    n = half * KT + k
                    if n >= 8:
                        pe.wait_ge(h_lo_done, n - 7)
                    for q in range(3):
                        t = 3 * half + q
                        if k == 0:
                            pe.wait_ge(x_scaled, t + 1)
                        last = nc.tensor.transpose(ps[:, n % 8, q * P:(q + 1) * P],
                                                   x_rows[t][:, k * P:(k + 1) * P], ident)
                    last.then_inc(xt_done, 1)

            def biases_by_distance():
                pe.wait_ge(hot_in, 32)
                pe.wait_ge(table_ones, 1)
                for n in range(2):
                    nc.tensor.matmul(ps[0:16, 4 + n, :], table, hot[:, n * 512:(n + 1) * 512],
                                     start=True, stop=True).then_inc(brow_ready, 1)

            def gemm_half(n, tile, parity, half):
                if half == 0 and (not isinstance(tile, int) or tile >= 2):
                    pe.wait_ge(tile_out, tile - 1)
                for c in (2 * half, 2 * half + 1):
                    pe.wait_ge(w_lo_done, n + c + 1)
                    for kk in range(KC):
                        k = c * KC + kk
                        w_h, w_l = (w[:, c, kk * P:(kk + 1) * P] for w in (w_hi, w_lo))
                        for p, (w, h) in enumerate(((w_h, h_hi), (w_h, h_lo), (w_l, h_hi))):
                            for b in range(2):
                                last = nc.tensor.matmul(
                                    ps[:, 2 * parity + b, 0:HALF_T], w,
                                    h[:, k * T + b * HALF_T:k * T + (b + 1) * HALF_T],
                                    start=(k == 0 and p == 0), stop=(k == KT - 1 and p == 2))
                                if k == KT - 1 and p == 2 and b == 1:
                                    last.then_inc(tile_done, 1)
                                    last = None
                    if last is not None:
                        last.then_inc(w_used, 1)

            def cb_prompt(g):
                pe.wait_ge(bc_silu, 2 * g + 2)
                for sc in range(PCH):
                    nc.tensor.matmul(ps[:, 4 + sc, :], bcT[0][:, sc * P:(sc + 1) * P], bcT[1][:, 0:SEQ],
                                     start=True, stop=True).then_inc(pcb_ready, 1)

            def cb_sample(g):
                pe.wait_ge(pcb_read, 5 * g + 1)
                for q in range(2):
                    last = nc.tensor.matmul(ps[:, 4, q * DEC_SEQ:(q + 1) * DEC_SEQ],
                                            bcT[0][:, SEQ + q * P:SEQ + (q + 1) * P], bcT[1][:, SEQ:T],
                                            start=True, stop=True)
                last.then_inc(pcb_ready, 1)

            def bc_tiles(g, post):
                for half in range(4):
                    gemm_half(2 * NCH * g + NCH * (half // 2), 2 * g + half // 2, half // 2, half % 2)
                    if post is None and half == 0:
                        pe.wait_ge(h_lo_done, 2 * KT)
                        biases_by_distance()
                    if post is not None and half == 2:
                        cb_prompt(post)
                    if post is not None and half == 3:
                        cb_sample(post)

            pe.wait_ge(h_lo_done, KT + 10)
            bc_tiles(0, None)
            with pe.Fori(0, SSM_GROUPS - 1) as g:
                bc_tiles(g + 1, g)
            for half in range(2):
                gemm_half(2 * NCH * SSM_GROUPS, PRO_TILES - 1, 0, half)

            def dt_transposes():
                pe.wait_ge(dt_out, 1)
                pe.wait_ge(pcb_read, 5 * (SSM_GROUPS - 1) + 2)
                for c in range(TT):
                    last = nc.tensor.transpose(ps[:, 5, c * 64:(c + 1) * 64], dtT[:, c * P:(c + 1) * P],
                                               ident[0:64, 0:64])
                last.then_inc(dtt_ready, 1)

            def dt_cumulate():
                pe.wait_ge(adt_ready, 1)
                pe.wait_ge(pcb_read, 5 * SSM_GROUPS)
                adt3 = adt.rearrange("p (c n) -> p c n", c=TT)
                loc3 = ps[:, 4, 0:W6].rearrange("p (c n) -> p c n", c=TT)
                for d in range(2):
                    last = nc.tensor.matmul(loc3[:, :, 32 * d:32 * d + 32], tri_incl[d],
                                            adt3[:, :, 32 * d:32 * d + 32], start=(d == 0), stop=True,
                                            skip_group_check=True)
                last.then_inc(cum_ready, 1)
                for c in range(TT):
                    for d in range(2):
                        b, o = (5, c) if c < PCH else (6, c - PCH)
                        last = nc.tensor.matmul(ps[32 * d:32 * d + 32, b, o * P:(o + 1) * P],
                                                adt3[:, c, 32 * d:32 * d + 32], tri_incl[d],
                                                start=True, stop=True)
                last.then_inc(cum_ready, 1)
                for d, lc, sc0, n, pair0 in RUNS:
                    for q in range(n):
                        sc = sc0 + q
                        out = ps[:, 7, (pair0 + q) * 32:(pair0 + q + 1) * 32]
                        mids = range(sc + 1, lc) if d == 0 else range(lc + 1, sc)
                        last = nc.tensor.matmul(out, tri_strict[d], adt3[:, sc, 32 * d:32 * d + 32],
                                                start=True, stop=(len(mids) == 0))
                        for m in mids:
                            last = nc.tensor.matmul(out, ones, adt3[:, m, 32 * d:32 * d + 32],
                                                    start=False, stop=(m == mids[-1]))
                last.then_inc(cum_ready, 1)

            QK_PASSES = ((q_hi, k_hi), (q_hi, k_lo), (q_lo, k_hi))

            def slot(s, a, i):
                if a is not None and s == 0:
                    pe.wait_ge(tile_out, PRO_TILES + TILES * a + K + 1)
                    pe.wait_ge(vt_out, 2 * a + 2)
                    for t in range(PCH):
                        for n, (q, k) in enumerate(QK_PASSES):
                            last = nc.tensor.matmul(ps[:, 4 + t, :], q[:, t * P:(t + 1) * P], k[:, 0:SEQ],
                                                    start=(n == 0), stop=(n == 2))
                        last.then_inc(scores_ready, 1)
                if a is not None and s == 1:
                    pe.wait_ge(biased, 6 * a + 1)
                    for t in range(2):
                        for n, (q, k) in enumerate(QK_PASSES):
                            last = nc.tensor.matmul(ps[:, 4, t * DEC_SEQ:(t + 1) * DEC_SEQ],
                                                    q[:, SEQ + t * P:SEQ + (t + 1) * P], k[:, SEQ:T],
                                                    start=(n == 0), stop=(n == 2))
                    last.then_inc(sscores_ready, 1)
                if a is not None and s == 2:
                    pe.wait_ge(normed, 6 * a + 4)
                    pe.wait_ge(biased, 6 * a + 6)
                    for b in range(PCH):
                        for t in range(PCH):
                            last = nc.tensor.transpose(ps[:, 4 + b, t * P:(t + 1) * P],
                                                       probs[:, t * SEQ + b * P:t * SEQ + (b + 1) * P], ident)
                        last.then_inc(pt_ready, 1)
                if a is not None and s == 3:
                    pe.wait_ge(normed, 6 * a + 6)
                    pe.wait_ge(pt_out_act, 2 * a + 1)
                    for b in range(2):
                        for t in range(2):
                            o = b * DEC_SEQ
                            last = nc.tensor.transpose(
                                ps[:, 4, o + t * P:o + (t + 1) * P],
                                probs_s[:, t * DEC_SEQ + b * P:t * DEC_SEQ + (b + 1) * P], ident)
                    last.then_inc(pts_ready, 1)
                if a is not None and s == 4:
                    pe.wait_ge(pt_out_act, 2 * a + 2)
                    pe.wait_ge(pt_out_dve, 2 * a + 2)
                    for b in range(PCH):
                        last = nc.tensor.matmul(ps[:, 5, :], v_tok[:, b * P:(b + 1) * P],
                                                pT[:, b * SEQ:(b + 1) * SEQ], start=(b == 0), stop=(b == PCH - 1))
                    last.then_inc(pv_ready, 1)
                    pe.wait_ge(pts_out, a + 1)
                    for b in range(2):
                        last = nc.tensor.matmul(ps[:, 6, 0:DEC_SEQ], v_tok[:, SEQ + b * P:SEQ + (b + 1) * P],
                                                pT_s[:, b * DEC_SEQ:(b + 1) * DEC_SEQ],
                                                start=(b == 0), stop=(b == 1))
                    last.then_inc(pv_ready, 1)
                if a is not None and s == 5:
                    pe.wait_ge(xs_silu, a + 1)
                    for half, bank in ((0, 7), (1, 4)):
                        for q in range(3):
                            c = 3 * half + q
                            last = nc.tensor.transpose(ps[:, bank, q * P:(q + 1) * P],
                                                       xsT[:, c * P:(c + 1) * P], ident)
                        last.then_inc(xt_ready, 1)
                if a is not None and s == 7:
                    pe.wait_ge(o_out, 2 * a + 2)
                    pe.wait_ge(xsc_done, a + 1)
                    pe.wait_ge(cb_in, 16 * a + 16)
                    for d, (bp, bs) in enumerate(((5, 6), (7, 4))):
                        for rd, lc, sc0, n, pair0 in RUNS:
                            if rd != d:
                                continue
                            b, o = (bp, lc) if lc < PCH else (bs, lc - PCH)
                            for q in range(n):
                                pr = pair0 + q
                                last = nc.tensor.matmul(ps[:, b, o * P:(o + 1) * P], xsc[:, pr * P:(pr + 1) * P],
                                                        cb[:, pr * P:(pr + 1) * P], start=(q == 0),
                                                        stop=(q == n - 1))
                        last.then_inc(off_ready, 1)
                if a is not None and s == 9:
                    pe.wait_ge(off_read, 2 * a + 1)
                    pe.wait_ge(wmat_done, a + 1)
                    for c in range(TT):
                        b, o = (5, c) if c < PCH else (6, c - PCH)
                        for h in range(2):
                            last = nc.tensor.matmul(
                                ps[64 * h:64 * h + 64, b, o * P:(o + 1) * P],
                                x_tok[:, c * P + 64 * h:c * P + 64 * h + 64],
                                decay[:, h * T + c * P:h * T + (c + 1) * P], start=True, stop=True)
                        if c in (PCH - 1, TT - 1):
                            last.then_inc(diag_ready, 1)
                if a is not None and s == 11:
                    pe.wait_ge(y_gated, a + 1)
                if i is not None and s == 10:
                    pe.wait_ge(tile_out, tile_of(i, V) + 1)
                    if a is not None:
                        pe.wait_ge(off_read, 2 * a + 2)
                    else:
                        pe.wait_ge(coef_exp, 1)
                        pe.wait_ge(loc_read, 1)
                    for half, bank in ((0, 7), (1, 4)):
                        for q in range(3):
                            c = 3 * half + q
                            last = nc.tensor.transpose(ps[:, bank, q * P:(q + 1) * P],
                                                       vT[:, c * P:(c + 1) * P], ident)
                        last.then_inc(vt_ready, 1)

            def iteration(i, a):
                for s in range(2 * TILES):
                    j, half = divmod(s, 2)
                    gemm_half(chunk_of(i, NCH * j), tile_of(i, j), (1 + j) % 2, half)
                    if a is None and s == 0:
                        cb_prompt(SSM_GROUPS - 1)
                    if a is None and s == 1:
                        cb_sample(SSM_GROUPS - 1)
                        dt_transposes()
                    if a is None and s == 5:
                        dt_cumulate()
                    slot(s, a, i)

            iteration(0, None)
            with pe.Fori(0, HEADS - 1) as a:
                iteration(a + 1, a)

            def part(par, slot, bank, t):
                for k in range(GRP):
                    for p, (m, w) in enumerate(((m_hi, w2_hi), (m_hi, w2_lo), (m_lo, w2_hi))):
                        last = nc.tensor.matmul(
                            ps[:, bank, :], m[par][:, k * T + t * P:k * T + (t + 1) * P],
                            w[slot][:, k * NBW:(k + 1) * NBW],
                            start=(k == 0 and p == 0), stop=(k == GRP - 1 and p == 2))
                last.then_inc(part_ready, 1)

            def sums_of_squares(step):
                pe.wait_ge(ssum_ready, step + 1)
                for t in range(TT):
                    last = nc.tensor.matmul(ps[:, 6, t:t + 1], ssum[:, t * P:(t + 1) * P], ones[:, 0:1],
                                            start=True, stop=True)
                last.then_inc(stat_ready, 1)

            def out_unit(step, par, unit, nb):
                pe.wait_ge(w2_lo_done, unit + 1)
                for t in range(TT):
                    pe.wait_ge(acc_added, (unit - 1) * TT + (t + 1))
                    part(par, nb % 2, t, t)

            def out_pair(pair):
                for par in range(2):
                    step = pair * 2 + par
                    if not (isinstance(step, int) and step == 0):
                        sums_of_squares(step)
                        pe.wait_ge(m_lo_done, GRP * step + GRP)
                    if isinstance(step, int) and step == STEPS - 1:
                        for n, (nb, t) in enumerate(LAST_ORDER):
                            pe.wait_ge(w2_lo_done, UNITS - NB + nb + 1)
                            pe.wait_ge(acc_added, TT * (UNITS - NB - 1) + n + 1)
                            part(par, w2_slot(UNITS - NB + nb), n % TT, t)
                        continue
                    for nb in range(NB):
                        unit = pair * (2 * NB) + (par * NB + nb)
                        if not (isinstance(unit, int) and unit == 0):
                            out_unit(step, par, unit, nb)

            for s in range(2 * TILES):
                slot(s, HEADS - 1, None)
                if s == 5:
                    pe.wait_ge(tile_out, PRO_TILES + TILES * HEADS)
                    pe.wait_ge(m_lo_done, GRP)
                    pe.wait_ge(w2_lo_done, 1)
                    part(0, 0, 0, 0)
                    part(0, 0, 1, 1)
                if s == 7:
                    part(0, 0, 2, 2)
                if s == 9:
                    part(0, 0, 3, 3)
            sums_of_squares(0)
            part(0, 0, 4, 4)
            part(0, 0, 5, 5)
            out_pair(0)
            with pe.Fori(1, STEPS // 2 - 1) as pair:
                out_pair(pair)
            out_pair(STEPS // 2 - 1)

        @block.scalar
        def _(act):
            def root_of_x(t):
                act.wait_ge(x_in[t], 16)
                if t:
                    act.wait_ge(x_squared, t)
                nc.scalar.activation(x_junk, x_rows[t], ACT.Square, accum_out=ssq[:, t:t + 1]).then_inc(x_squared, 1)
                act.wait_ge(x_ms, t + 1)
                nc.scalar.activation(rx[:, t:t + 1], ssq[:, t:t + 1], ACT.Sqrt).then_inc(x_root, 1)

            def split_hi(n, c, tile):
                act.wait_ge(w_in_s[c], 16 * tile + 16)
                if not isinstance(n, int) or n >= NCH:
                    if c == NCH - 1:
                        act.wait_ge(tile_done, tile)
                    else:
                        act.wait_ge(w_used, tile * (NCH - 1) + (c + 2 - NCH))
                nc.scalar.activation(w_hi[:, c, :], w_raw[:, c, :], ACT.Copy).then_inc(w_hi_done, 1)

            def tile_ready(tile):
                act.wait_ge(tile_done, tile + 1)

            def tile_into(tile, parity, dst, func=ACT.Copy, scale=1.0):
                nc.scalar.activation(dst.rearrange("p (b t) -> p b t", b=2),
                                     ps[:, 2 * parity:2 * parity + 2, 0:HALF_T], func, scale=scale
                                     ).then_inc(tile_out, 1)

            def tile_hi(parity, dst, scale):
                nc.scalar.activation(dst[:, :].rearrange("p (b t) -> p b t", b=2),
                                     ps[:, 2 * parity:2 * parity + 2, 0:HALF_T], ACT.Copy, scale=scale
                                     ).then_inc(qk_hi_done, 1)

            def tile_padded(parity, dst):
                nc.scalar.activation(dst[:, 2:2 + HALF_T], ps[:, 2 * parity, 0:HALF_T], ACT.Copy)
                nc.scalar.activation(dst[:, 2 + HALF_T:2 + SEQ], ps[:, 2 * parity + 1, 0:SEQ - HALF_T], ACT.Copy)
                nc.scalar.activation(dst[:, 6 + SEQ:6 + T], ps[:, 2 * parity + 1, SEQ - HALF_T:HALF_T], ACT.Copy
                                     ).then_inc(tile_out, 1)

            def silu(dst, src, done):
                nc.scalar.activation(dst[:, 0:SEQ], src[:, 0:SEQ], ACT.Silu)
                nc.scalar.activation(dst[:, SEQ:T], src[:, SEQ + 4:T + 4], ACT.Silu).then_inc(done, 1)

            for t in range(4):
                root_of_x(t)
            for h in range(2):
                act.dma_start(skip_cols[64 * h:64 * h + 64, :],
                              d_skip[0].rearrange("(t h) -> h t", h=2)[h:h + 1, :].partition_broadcast(64)
                              .rearrange("p a b -> p (a b)"), allow_slow_non_contiguous=True).then_inc(skip_in, 16)
            act.wait_ge(cols_read, 2)
            for n in range(2 * KT):
                if n in X_TURNS:
                    root_of_x(X_TURNS[n])
                half, k = divmod(n, KT)
                o = k * T + half * HALF_T
                act.wait_ge(xt_done, n + 1)
                nc.scalar.activation(h_hi[:, o:o + HALF_T], ps[:, n % 8, 0:HALF_T], ACT.Copy,
                                     scale=pre_cols[:, k:k + 1]).then_inc(h_hi_done, 1)
                for c in W_TURNS.get(n, ()):
                    split_hi(c, c, 0)

            def bc_steps(g, post):
                for s in range(4):
                    for m in (2 * s + 4, 2 * s + 5):
                        split_hi(2 * NCH * g + m, m % NCH, 2 * g + m // NCH)
                    if s == 1:
                        tile_ready(2 * g)
                        if post is not None:
                            act.wait_ge(bc_conved, 2 * post + 1)
                        else:
                            act.wait_ge(pads, 2)
                        tile_padded(0, bc_raw[0])
                        if post is not None:
                            silu(bcT[0], bc_conv[0], bc_silu)
                            act.wait_ge(bc_conved, 2 * post + 2)
                            silu(bcT[1], bc_conv[1], bc_silu)
                    if s == 3:
                        tile_ready(2 * g + 1)
                        tile_padded(1, bc_raw[1])
                        if post is not None:
                            store_cb(post)
                            act.wait_ge(cb_stored, 16 * post + 16)

            def store_cb(g):
                act.wait_ge(pcb_read, 5 * g + 5)
                act.dma_start(cb_scr[ds(g * P, P), :], cb).then_inc(cb_stored, 16)

            bc_steps(0, None)
            with act.Fori(0, SSM_GROUPS - 1) as g:
                bc_steps(g + 1, g)
            last = SSM_GROUPS - 1
            dt_n = 2 * NCH * SSM_GROUPS
            for s in range(2):
                for m in (2 * s + 4, 2 * s + 5):
                    split_hi(dt_n + m, m % NCH, PRO_TILES - 1 + m // NCH)
                if s == 1:
                    act.wait_ge(bc_conved, 2 * last + 1)
                    silu(bcT[0], bc_conv[0], bc_silu)
                    act.wait_ge(bc_conved, 2 * last + 2)
                    silu(bcT[1], bc_conv[1], bc_silu)
                    tile_ready(PRO_TILES - 1)
                    for b in range(2):
                        out = nc.scalar.activation(dtT[:, b * HALF_T:(b + 1) * HALF_T], ps[0:64, b, 0:HALF_T], ACT.Copy)
                        if b:
                            out.then_inc(dt_out, 1)
            act.wait_ge(dt_out, 1)
            nc.scalar.activation(cur[0:1, 120:121], cur[0:1, 114:115], ACT.Copy).then_inc(tile_out, 1)

            def silu_of_xs(a):
                act.wait_ge(conved, a + 1)
                silu(xsT, conv, xs_silu)

            def exp_of_decays(a):
                act.wait_ge(decay_arg, a + 1)
                nc.scalar.activation(decay, decay, ACT.Exp).then_inc(decay_exp, 1)

            def step(s, a, i):
                if a is not None and s == 0:
                    act.wait_ge(negmax, 2 * a + 1)
                    for t in range(PCH):
                        nc.scalar.activation(probs[:, t * SEQ:(t + 1) * SEQ], probs[:, t * SEQ:(t + 1) * SEQ], ACT.Exp,
                                             bias=nmx[:, t:t + 1], accum_out=lsum[:, t:t + 1]).then_inc(probs_exp, 1)
                if i is not None and s == 1:
                    tile_ready(tile_of(i, V))
                    tile_into(tile_of(i, V), 1, vT)
                if a is not None and s == 1:
                    act.wait_ge(negmax, 2 * a + 2)
                    for t in range(2):
                        nc.scalar.activation(probs_s[:, t * DEC_SEQ:(t + 1) * DEC_SEQ],
                                             probs_s[:, t * DEC_SEQ:(t + 1) * DEC_SEQ], ACT.Exp,
                                             bias=nmx[:, PCH + t:PCH + t + 1],
                                             accum_out=lsum[:, PCH + t:PCH + t + 1]).then_inc(probs_exp, 1)
                if a is not None and s == 2:
                    for b in range(2):
                        act.wait_ge(pt_ready, 4 * a + b + 1)
                        nc.scalar.activation(pT[:, b * SEQ:(b + 1) * SEQ], ps[:, 4 + b, :], ACT.Copy
                                             ).then_inc(pt_out_act, 1)
                if i is not None and s == 3:
                    tile_ready(tile_of(i, Q))
                    if a is not None:
                        act.wait_ge(sscores_ready, a + 1)
                    tile_hi(0, q_hi, Q_SCALE)
                if a is not None and s == 3:
                    act.wait_ge(pts_ready, a + 1)
                    nc.scalar.activation(pT_s, ps[:, 4, :], ACT.Copy).then_inc(pts_out, 1)
                    if i is not None:
                        silu_of_xs(a)
                if a is not None and s == 4:
                    act.wait_ge(pv_ready, 2 * a + 1)
                    nc.scalar.activation(oT[:, 0:SEQ], ps[:, 5, :], ACT.Copy).then_inc(o_out, 1)
                    act.wait_ge(pv_ready, 2 * a + 2)
                    nc.scalar.activation(oT[:, SEQ:T], ps[:, 6, 0:DEC_SEQ], ACT.Copy).then_inc(o_out, 1)
                    act.wait_ge(o_out, 2 * a + 2)
                    act.wait_ge(xs_silu, a + 1)
                    nc.scalar.activation(sqT[:, 0:T], oT, ACT.Square).then_inc(o_sq, 1)
                if i is not None and s == 5:
                    tile_ready(tile_of(i, K))
                    tile_hi(1, k_hi, 1.0)
                if a is not None and s == 5:
                    for half, bank in ((0, 7), (1, 4)):
                        act.wait_ge(xt_ready, 2 * a + half + 1)
                        nc.scalar.activation(x_tok[:, half * HALF_T:(half + 1) * HALF_T], ps[:, bank, 0:HALF_T],
                                             ACT.Copy).then_inc(xt_out, 1)
                    act.wait_ge(att_gated, a + 1)
                    act.dma_start(u_scr[ds(a * P, P), :], oT).then_inc(ua_stored, 16)
                if a is not None and i is not None and s == 6:
                    exp_of_decays(a)
                if i is not None and s == 7:
                    tile_ready(tile_of(i, ZA))
                    act.wait_ge(tile_out, tile_of(i, K) + 1)
                    tile_into(tile_of(i, ZA), 0, za, func=ACT.Silu)
                if a is not None and s == 8:
                    act.wait_ge(ua_stored, 16 * a + 16)
                if i is not None and s == 9:
                    tile_ready(tile_of(i, XS))
                    if a is None:
                        act.wait_ge(pads, 3)
                    tile_padded(1, xs_raw)
                if a is not None and s == 10:
                    act.wait_ge(y_gated, a + 1)
                    act.dma_start(u_scr[ds((a + HEADS) * P, P), :], y).then_inc(ys_stored, 16)
                if i is not None and s == 10:
                    for half, bank in ((0, 7), (1, 4)):
                        act.wait_ge(vt_ready, 2 * i + half + 1)
                        nc.scalar.activation(v_tok[:, half * HALF_T:(half + 1) * HALF_T], ps[:, bank, 0:HALF_T],
                                             ACT.Copy).then_inc(vt_out, 1)
                if i is not None and s == 11:
                    tile_ready(tile_of(i, ZS))
                    tile_into(tile_of(i, ZS), 0, zs, func=ACT.Silu)

            def dt_step(s):
                if s == 1:
                    store_cb(last)
                    act.wait_ge(row_in, 64)
                    nc.scalar.activation(a_row, a_row, ACT.Exp).then_inc(a_exp, 1)
                    act.wait_ge(dt_exp_arg, 1)
                    nc.scalar.activation(du, du, ACT.Exp).then_inc(dt_exp, 1)
                if s == 5:
                    act.wait_ge(cum_ready, 2)
                    nc.scalar.activation(loc_rows[:, 0:SEQ], ps[0:64, 5, :], ACT.Copy).then_inc(rows_read, 1)
                    nc.scalar.activation(loc_rows[:, SEQ:T], ps[0:64, 6, 0:DEC_SEQ], ACT.Copy).then_inc(rows_read, 1)
                    act.wait_ge(rows_read, 2)
                    nc.scalar.activation(er_rows, loc_rows, ACT.Exp).then_inc(rows_read, 1)
                    act.dma_start(loc_scr, loc_rows).then_inc(rows_stored, 16)
                    act.wait_ge(rows_read, 3)
                    act.dma_start(er_scr, er_rows).then_inc(rows_stored, 16)
                    act.wait_ge(cum_ready, 3)
                    nc.scalar.activation(coef[:, :], ps[:, 7, 0:PAIRS * 32], ACT.Exp).then_inc(coef_exp, 1)

            def iteration(i, a, final=False):
                for s in range(2 * TILES):
                    for m in (2 * s + 4, 2 * s + 5):
                        if not (final and m >= IT_CHUNKS):
                            split_hi(chunk_of(i, m), m % NCH, tile_of(i, m // NCH))
                    if a is None:
                        dt_step(s)
                    step(s, a, i)
                    if final and s == 10:
                        silu_of_xs(i)
                        exp_of_decays(i)

            iteration(0, None)
            with act.Fori(0, HEADS - 2) as a:
                iteration(a + 1, a)
            iteration(HEADS - 1, HEADS - 2, final=True)
            def w2_split(u):
                act.wait_ge(w2_in[u % 2], 16 * (u // 2 + 1))
                if 2 <= u < UNITS - 2:
                    act.wait_ge(part_ready, TT * (u - 1))
                if u == UNITS - 1:
                    act.wait_ge(part_ready, TT * (UNITS - NB))
                nc.scalar.activation(w2_hi[w2_slot(u)], w2_raw[u % 2] if u >= 2 else w2_first, ACT.Copy
                                     ).then_inc(w2_hi_done, 1)

            def m_split_first(k):
                act.wait_ge(u_first_in[k], 16)
                kt = STEP_GROUPS[0] * GRP + k
                nc.scalar.activation(m_hi[0][:, k * T:(k + 1) * T], u_first[k], ACT.Copy,
                                     scale=mix_cols[:, kt:kt + 1]).then_inc(m_hi_done, 1)
                if k == 0:
                    return
                act.wait_ge(usq_added, k)
                nc.scalar.activation(usq_first, u_first[k], ACT.Square).then_inc(usq_done, 1)

            act.wait_ge(tile_done, PRO_TILES + TILES * HEADS)
            w2_split(0)
            for s in range(2 * TILES):
                step(s, HEADS - 1, None)
                if s == 1:
                    m_split_first(0)
                if s == 3:
                    for k in range(1, GRP):
                        m_split_first(k)
                if s == 6:
                    w2_split(1)

            def m_split(s, k):
                if k == 0:
                    act.wait_ge(u_in, 16 * s)
                    if s >= 2:
                        act.wait_ge(part_ready, TT * NB * (s - 1))
                kt = STEP_GROUPS[s] * GRP + k
                nc.scalar.activation(m_hi[s % 2][:, k * T:(k + 1) * T], u_raw[:, k * T:(k + 1) * T], ACT.Copy,
                                     scale=mix_cols[:, kt:kt + 1]).then_inc(m_hi_done, 1)
                if s < 4 and k:
                    act.wait_ge(ssum_ready, s)
                    act.wait_ge(usq_added, (GRP - 1) * s + k)
                    nc.scalar.activation(usq, u_raw[:, k * T:(k + 1) * T], ACT.Square).then_inc(usq_done, 1)

            for s in range(STEPS):
                act.wait_ge(stat_read, s + 1)
                nc.scalar.activation(r_cur[:, s % 2, :], r_cur[:, s % 2, :], ACT.Sqrt).then_inc(r_root, 1)
                if s < STEPS - 1:
                    for nb in range(NB):
                        if s or nb:
                            w2_split(s * NB + nb + 1)
                        m_split(s + 1, nb)
            for n, (nb, t) in enumerate(LAST_ORDER):
                if nb == 0 and t < NB - 1:
                    w2_split(UNITS - NB + t + 1)
                o = t * D_MODEL + nb * NBW
                act.wait_ge(acc_added, TT * (UNITS - NB) + n + 1)
                if n:
                    act.wait_ge(fin_sq, n)
                nc.scalar.activation(fin_junk, acc[:, o:o + NBW], ACT.Square,
                                     accum_out=fin_parts[:, nb, t:t + 1]).then_inc(fin_sq, 1)
                if nb == NB - 1:
                    act.wait_ge(fin_ms, t + 1)
                    nc.scalar.activation(fin_rms[:, t:t + 1], fin_mean[:, t:t + 1], ACT.Sqrt).then_inc(fin_root, 1)

        @block.vector
        def _(dve):
            seq = [0, 0]

            def did(ins):
                ins.then_inc(dve_seq, 1)
                seq[1] += 1

            def settle():
                dve.wait_ge(dve_seq, seq[0] + seq[1])

            def copy(dst, src):
                return nc.vector.tensor_copy(dst, src)

            nc.vector.memset(table[32:33, :], 1.0).then_inc(table_ones, 1)
            did(nc.vector.memset(osq_sum[:, :], 0.0))

            def scale_x(t):
                dve.wait_ge(x_squared, t + 1)
                nc.vector.tensor_scalar(ssq[:, t:t + 1], ssq[:, t:t + 1], 1.0 / D_MODEL, EPS, ALU.mult, ALU.add
                                        ).then_inc(x_ms, 1)
                dve.wait_ge(x_root, t + 1)
                nc.vector.reciprocal(rx[:, t:t + 1], rx[:, t:t + 1]).then_inc(x_rinv, 1)
                dve.wait_ge(x_rinv, t + 1)
                nc.vector.tensor_scalar(x_rows[t], x_rows[t], rx[:, t:t + 1], None, ALU.mult).then_inc(x_scaled, 1)

            def split_lo(n, c):
                dve.wait_ge(w_hi_done, n + 1)
                nc.vector.tensor_tensor(w_lo[:, c, :], w_raw[:, c, :], w_hi[:, c, :].bitcast(f32), ALU.subtract
                                        ).then_inc(w_lo_done, 1)

            scale_x(0)
            dve.wait_ge(cols_ready, 1)
            copy(conv_cols[:, :], ps[:, 7, 0:120]).then_inc(cols_read, 1)
            copy(vec_cols[:, :], ps[:, 7, 128:200]).then_inc(cols_read, 1)
            for t in range(1, 4):
                scale_x(t)
            for n in range(2 * KT):
                if n in X_TURNS:
                    scale_x(X_TURNS[n])
                half, k = divmod(n, KT)
                o = k * T + half * HALF_T
                dve.wait_ge(h_hi_done, n + 1)
                nc.vector.scalar_tensor_tensor(h_lo[:, o:o + HALF_T], ps[:, n % 8, 0:HALF_T], pre_cols[:, k:k + 1],
                                               h_hi[:, o:o + HALF_T].bitcast(f32), ALU.mult, ALU.subtract
                                               ).then_inc(h_lo_done, 1)
                for c in W_TURNS.get(n, ()):
                    split_lo(c, c)

            def biases_out():
                for n in range(2):
                    dve.wait_ge(brow_ready, n + 1)
                    copy(brow[:, n * 512:(n + 1) * 512], ps[0:16, 4 + n, :]).then_inc(brow_read, 1)

            def zero_pads():
                dve.wait_ge(xt_done, 2 * KT)
                dve.wait_ge(brow_out, 16)
                for buf in (bc_raw[0], bc_raw[1], xs_raw):
                    nc.vector.memset(buf[:, 0:2], 0.0)
                    nc.vector.memset(buf[:, 2 + SEQ:6 + SEQ], 0.0)
                    nc.vector.memset(buf[:, 6 + T:8 + T], 0.0).then_inc(pads, 1)

            def convolve(dst, src, tap, bias, done):
                W = T + 4
                did(nc.vector.tensor_scalar(dst[:, 0:W], src[:, 0:W], tap(0), bias, ALU.mult, ALU.add))
                for k in range(1, CONV_W):
                    settle()
                    ins = nc.vector.scalar_tensor_tensor(dst[:, 0:W], src[:, k:k + W], tap(k), dst[:, 0:W],
                                                         ALU.mult, ALU.add)
                    if k < CONV_W - 1:
                        did(ins)
                    else:
                        ins.then_inc(done, 1)

            def bc_conv_step(g):
                taps = conv_cols[:, :].rearrange("p (k t) -> p k t", k=CONV_W)
                for q in range(2):
                    tile = 2 * g + q
                    ct = 16 + 4 * q + g
                    did(copy(tap_cur, taps[:, :, ds(ct, 1)].rearrange("p k t -> p (k t)")))
                    did(copy(bias_cur, convb_cols[:, ds(ct, 1)]))
                    settle()
                    dve.wait_ge(tile_out, 2 * g + 2)
                    convolve(bc_conv[q], bc_raw[q], lambda k: tap_cur[:, k:k + 1], bias_cur, bc_conved)
                    dve.wait_ge(bc_conved, 2 * g + q + 1)

            def cb_out(g, sample):
                own = cb[:, PAIRS * P:].rearrange("p (d c n) -> p d c n", d=2, c=TT)
                for bank in ((4,) if sample else (4, 5, 6, 7)):
                    dve.wait_ge(pcb_ready, 5 * g + (5 if sample else bank - 3))
                    srcs = (PCH, PCH + 1) if sample else (bank - 4,)
                    for sc in srcs:
                        base = (sc - PCH) * DEC_SEQ if sample else 0
                        first = PCH if sample else 0
                        for d in range(2):
                            o = base + (sc - first) * P
                            last = nc.vector.tensor_tensor(own[:, d, sc, :], ps[:, bank, o:o + P], tri_incl[d],
                                                           ALU.mult)
                        for d, lc, sc0, n, pair0 in RUNS:
                            if sc0 <= sc < sc0 + n:
                                pr, o = pair0 + sc - sc0, base + (lc - first) * P
                                last = copy(cb[:, pr * P:(pr + 1) * P], ps[:, bank, o:o + P])
                    last.then_inc(pcb_read, 1)

            def bc_steps(g, post):
                for s in range(4):
                    for m in (2 * s + 4, 2 * s + 5):
                        split_lo(2 * NCH * g + m, m % NCH)
                    if post is None:
                        if s == 0:
                            biases_out()
                        if s == 1:
                            zero_pads()
                    if post is not None:
                        if s == 0:
                            bc_conv_step(post)
                        if s == 2:
                            cb_out(post, False)
                        if s == 3:
                            cb_out(post, True)

            bc_steps(0, None)
            BC_SEQ = 12
            start = seq[1]
            with dve.Fori(0, SSM_GROUPS - 1) as g:
                seq[:] = [start + BC_SEQ * g, 0]
                bc_steps(g + 1, g)
                assert seq[1] == BC_SEQ, seq[1]
            seq[:] = [0, start + BC_SEQ * (SSM_GROUPS - 1)]
            last_g = SSM_GROUPS - 1
            dt_n = 2 * NCH * SSM_GROUPS
            for s in range(2):
                for m in (2 * s + 4, 2 * s + 5):
                    split_lo(dt_n + m, m % NCH)
                if s == 0:
                    bc_conv_step(last_g)
            dve.wait_ge(skip_in, 32)

            def tt(out, a, b, op):
                did(nc.vector.tensor_tensor(out, a, b, op))

            def dt_step(s):
                if s == 0:
                    cb_out(last_g, False)
                if s == 1:
                    cb_out(last_g, True)
                    dve.wait_ge(row_in, 64)
                    dve.wait_ge(dtt_ready, 1)
                    per_chunk = lambda t: t.rearrange("p (c n) -> p c n", c=TT)
                    tt(per_chunk(dx), per_chunk(ps[:, 5, 0:W6]),
                       dtb_row.unsqueeze(1).broadcast_to([P, TT, 64]), ALU.add)
                    settle()
                    nc.vector.scalar_tensor_tensor(du, dx, -1.0, dx, ALU.mult, ALU.min).then_inc(dt_exp_arg, 1)
                    dve.wait_ge(dt_exp, 1)
                    did(nc.vector.tensor_scalar(dz, du, 2.0, None, ALU.add))
                    settle()
                    did(nc.vector.reciprocal(dz, dz))
                    settle()
                    tt(dz, dz, du, ALU.mult)
                    settle()
                    tt(dz2, dz, dz, ALU.mult)
                    settle()
                    did(nc.vector.tensor_scalar(dp, dz2, 1.0 / 15.0, None, ALU.mult))
                    for n in (13, 11, 9, 7, 5, 3):
                        settle()
                        did(nc.vector.scalar_tensor_tensor(dp, dp, 1.0 / n, dz2, ALU.add, ALU.mult))
                    settle()
                    did(nc.vector.scalar_tensor_tensor(dp, dp, 1.0, dz, ALU.add, ALU.mult))
                    did(nc.vector.tensor_scalar(dx, dx, 0.0, None, ALU.max))
                    settle()
                    did(nc.vector.scalar_tensor_tensor(dt_cols[:, :], dp, 2.0, dx, ALU.mult, ALU.add))
                    dve.wait_ge(a_exp, 1)
                    settle()
                    nc.vector.scalar_tensor_tensor(
                        per_chunk(adt), per_chunk(dt_cols[:, :]), -1.0,
                        a_row.unsqueeze(1).broadcast_to([P, TT, 64]), ALU.mult, ALU.mult).then_inc(adt_ready, 1)
                if s == 5:
                    dve.wait_ge(cum_ready, 1)
                    copy(loc_cols[:, :], ps[:, 4, 0:W6]).then_inc(loc_read, 1)
                    dve.wait_ge(coef_exp, 1)
                    coef3 = coef[:, :].rearrange("p (r h) -> p r h", h=32)
                    dt3 = dt_cols[:, :].rearrange("p (c n) -> p c n", c=TT)
                    for d, lc, sc0, n, pair0 in RUNS:
                        tt(coef3[:, pair0:pair0 + n, :], coef3[:, pair0:pair0 + n, :],
                           dt3[:, sc0:sc0 + n, 32 * d:32 * d + 32], ALU.mult)
                    dve.wait_ge(loc_read, 1)
                    settle()

            def columns_of_channels(a):
                taps = conv_cols[:, :].rearrange("p (k t) -> p k t", k=CONV_W)
                did(copy(tap_cur, taps[:, :, ds(a, 1)].rearrange("p k t -> p (k t)")))
                did(copy(bias_cur, convb_cols[:, ds(a, 1)]))
                did(copy(skip_cur, skip_cols[:, ds(a, 1)]))

            def columns_of_heads(a):
                did(copy(coef_cur.rearrange("p (r h) -> p r h", h=2),
                         coef[:, :].rearrange("p (r h) -> p r h", h=32)[:, :, ds(a * 2, 2)]))
                for dst, src in ((loc_cur, loc_cols), (dt_cur, dt_cols)):
                    for d in range(2):
                        did(copy(dst[:, 12 * d:12 * d + 12].rearrange("p (h c) -> p c h", h=2),
                                 src[:, :].rearrange("p (c n) -> p c n", c=TT)[:, :, ds(a * 2 + 32 * d, 2)]))

            def convolve_xs(a):
                dve.wait_ge(tile_out, PRO_TILES + TILES * a + XS + 1)
                convolve(conv, xs_raw, lambda k: tap_cur[:, k:k + 1], bias_cur, conved)

            def decay_exponents(a):
                dve.wait_ge(decay_in, 16 * a + 16)
                dv = decay.rearrange("p (r n) -> p r n", n=P)
                tt(dv, dv, loc_cur.unsqueeze(2).broadcast_to([P, 24, P]), ALU.subtract)
                settle()
                nc.vector.tensor_scalar(decay, decay, 0.0, None, ALU.min).then_inc(decay_arg, 1)

            def decay_times_dt(a):
                dve.wait_ge(decay_exp, a + 1)
                dv = decay.rearrange("p (r n) -> p r n", n=P)
                tt(dv, dv, dt_cur.unsqueeze(2).broadcast_to([P, 24, P]), ALU.mult)

            def weights_in_chunks(a):
                settle()
                dve.wait_ge(cb_in, 16 * a + 16)
                for d in range(2):
                    part = decay[:, 2 * T * d:2 * T * (d + 1)].rearrange("p (h n) -> p h n", h=2)
                    own = cb[:, PAIRS * P + T * d:PAIRS * P + T * (d + 1)]
                    tt(part, part, own.unsqueeze(1).broadcast_to([P, 2, T]), ALU.mult)
                settle()
                nc.vector.tensor_tensor(decay[:, 0:2 * T], decay[:, 0:2 * T], decay[:, 2 * T:4 * T], ALU.add
                                        ).then_inc(wmat_done, 1)

            def tile_lo(n, parity, lo, hi, scale):
                dve.wait_ge(qk_hi_done, n + 1)
                nc.vector.scalar_tensor_tensor(
                    lo[:, :].rearrange("p (b t) -> p b t", b=2), ps[:, 2 * parity:2 * parity + 2, 0:HALF_T], scale,
                    hi[:, :].bitcast(f32).rearrange("p (b t) -> p b t", b=2), ALU.mult, ALU.subtract
                    ).then_inc(tile_out, 1)

            def step(s, a, i):
                if i is not None and s == 3:
                    tile_lo(2 * i, 0, q_lo, q_hi, Q_SCALE)
                if i is not None and s == 5:
                    tile_lo(2 * i + 1, 1, k_lo, k_hi, 1.0)
                if a is None:
                    return
                if s == 0 and i is None:
                    dve.wait_ge(scores_ready, PCH * a + PCH)
                    dve.wait_ge(strip_in, 16 * a + 16)
                if s == 0 and i is not None:
                    columns_of_channels(a)
                    dve.wait_ge(scores_ready, PCH * a + PCH)
                    dve.wait_ge(strip_in, 16 * a + 16)
                    columns_of_heads(a)
                if s == 0:
                    for t in range(PCH):
                        o = SEQ - P - t * P
                        nc.vector.tensor_tensor_reduce(
                            out=probs[:, t * SEQ:(t + 1) * SEQ], in0=ps[:, 4 + t, :], in1=strip[:, o:o + SEQ],
                            scale=1.0, scalar=-3e38, op0=ALU.add, op1=ALU.max,
                            accum_out=mx[:, t:t + 1]).then_inc(biased, 1)
                    dve.wait_ge(biased, 6 * a + 4)
                    nc.vector.tensor_scalar(nmx[:, 0:4], mx[:, 0:4], -1.0, None, ALU.mult).then_inc(negmax, 1)
                if s == 1:
                    dve.wait_ge(sscores_ready, a + 1)
                    dve.wait_ge(probs_exp, 6 * a + 4)
                    did(nc.vector.reciprocal(rinv[:, 0:4], lsum[:, 0:4]))
                    for t in range(2):
                        o = SEQ - P - t * P
                        nc.vector.tensor_tensor_reduce(
                            out=probs_s[:, t * DEC_SEQ:(t + 1) * DEC_SEQ],
                            in0=ps[:, 4, t * DEC_SEQ:(t + 1) * DEC_SEQ], in1=strip[:, o:o + DEC_SEQ],
                            scale=1.0, scalar=-3e38, op0=ALU.add, op1=ALU.max,
                            accum_out=mx[:, 4 + t:5 + t]).then_inc(biased, 1)
                    dve.wait_ge(biased, 6 * a + 6)
                    nc.vector.tensor_scalar(nmx[:, 4:6], mx[:, 4:6], -1.0, None, ALU.mult).then_inc(negmax, 1)
                    settle()
                    for t in range(PCH):
                        nc.vector.tensor_scalar(probs[:, t * SEQ:(t + 1) * SEQ], probs[:, t * SEQ:(t + 1) * SEQ],
                                                rinv[:, t:t + 1], None, ALU.mult).then_inc(normed, 1)
                if s == 2:
                    dve.wait_ge(probs_exp, 6 * a + 6)
                    did(nc.vector.reciprocal(rinv[:, 4:6], lsum[:, 4:6]))
                    settle()
                    for t in range(2):
                        nc.vector.tensor_scalar(probs_s[:, t * DEC_SEQ:(t + 1) * DEC_SEQ],
                                                probs_s[:, t * DEC_SEQ:(t + 1) * DEC_SEQ],
                                                rinv[:, 4 + t:5 + t], None, ALU.mult).then_inc(normed, 1)
                    for b in (2, 3):
                        dve.wait_ge(pt_ready, 4 * a + b + 1)
                        copy(pT[:, b * SEQ:(b + 1) * SEQ], ps[:, 4 + b, :]).then_inc(pt_out_dve, 1)
                    if i is not None:
                        convolve_xs(a)
                if s == 4:
                    dve.wait_ge(o_sq, a + 1)
                    tt(osq_sum[:, :], osq_sum[:, :], sqT[:, 0:T], ALU.add)
                    settle()
                    nc.vector.tensor_tensor(oT, oT, za, ALU.mult).then_inc(att_gated, 1)
                if s == 5:
                    dve.wait_ge(xt_out, 2 * a + 2)
                    dve.wait_ge(pv_ready, 2 * a + 1)
                    for d, lc, sc0, n, pair0 in RUNS:
                        ins = nc.vector.tensor_tensor(
                            xsc[:, pair0 * P:(pair0 + n) * P].rearrange("p (r n) -> p r n", n=64),
                            x_tok[:, sc0 * P:(sc0 + n) * P].rearrange("p (r n) -> p r n", n=64),
                            coef_cur[:, 2 * pair0:2 * (pair0 + n)].unsqueeze(2).broadcast_to([P, 2 * n, 64]),
                            ALU.mult)
                    ins.then_inc(xsc_done, 1)
                    if i is not None:
                        decay_exponents(a)
                if s == 6 and i is not None:
                    decay_times_dt(a)
                    weights_in_chunks(a)
                if s == 7:
                    dve.wait_ge(xs_silu, a + 1)
                    did(nc.vector.tensor_scalar(y, xsT, skip_cur, None, ALU.mult))
                    dve.wait_ge(er_in, 32 * a + 32)
                    for d, bp, bs, p0, p1, q0 in ((0, 5, 6, P, SEQ, P), (1, 7, 4, 0, SEQ - P, 0)):
                        dve.wait_ge(off_ready, 2 * a + d + 1)
                        tt(ytmp[:, p0:p1], ps[:, bp, p0:p1], er[:, d * T + p0:d * T + p1], ALU.mult)
                        nc.vector.tensor_tensor(ytmp[:, SEQ + q0:SEQ + q0 + P], ps[:, bs, q0:q0 + P],
                                                er[:, d * T + SEQ + q0:d * T + SEQ + q0 + P], ALU.mult
                                                ).then_inc(off_read, 1)
                        settle()
                        tt(y[:, p0:p1], y[:, p0:p1], ytmp[:, p0:p1], ALU.add)
                        dve.wait_ge(off_read, 2 * a + d + 1)
                        tt(y[:, SEQ + q0:SEQ + q0 + P], y[:, SEQ + q0:SEQ + q0 + P],
                           ytmp[:, SEQ + q0:SEQ + q0 + P], ALU.add)
                        settle()
                if s == 9:
                    dve.wait_ge(diag_ready, 2 * a + 1)
                    tt(y[:, 0:SEQ], y[:, 0:SEQ], ps[:, 5, :], ALU.add)
                    dve.wait_ge(diag_ready, 2 * a + 2)
                    tt(y[:, SEQ:T], y[:, SEQ:T], ps[:, 6, 0:DEC_SEQ], ALU.add)
                    settle()
                    dve.wait_ge(tile_out, PRO_TILES + TILES * a + ZS + 1)
                    nc.vector.tensor_tensor(y, y, zs, ALU.mult).then_inc(y_gated, 1)
                if s == 11:
                    dve.wait_ge(ys_stored, 16 * a + 16)
                    dve.wait_ge(ua_stored, 16 * a + 16)

            def iteration(i, a, final=False):
                for s in range(2 * TILES):
                    for m in (2 * s + 4, 2 * s + 5):
                        if not (final and m >= IT_CHUNKS):
                            split_lo(chunk_of(i, m), m % NCH)
                    if a is None:
                        dt_step(s)
                    step(s, a, i)
                    if final and s == 9:
                        dve.wait_ge(y_gated, i)
                        columns_of_channels(i)
                        columns_of_heads(i)
                        settle()
                        convolve_xs(i)
                        decay_exponents(i)

            iteration(0, None)
            start = seq[1]
            with dve.Fori(0, HEADS - 2) as a:
                seq[:] = [start + DVE_PER_PASS * a, 0]
                iteration(a + 1, a)
                assert seq[1] == DVE_PER_PASS, seq[1]
            seq[:] = [0, start + DVE_PER_PASS * (HEADS - 2)]
            iteration(HEADS - 1, HEADS - 2, final=True)
            def w2_split(u):
                dve.wait_ge(w2_hi_done, u + 1)
                nc.vector.tensor_tensor(w2_lo[w2_slot(u)], w2_raw[u % 2] if u >= 2 else w2_first,
                                        w2_hi[w2_slot(u)].bitcast(f32),
                                        ALU.subtract).then_inc(w2_lo_done, 1)

            def m_split_first(k):
                dve.wait_ge(m_hi_done, k + 1)
                kt = STEP_GROUPS[0] * GRP + k
                nc.vector.scalar_tensor_tensor(
                    m_lo[0][:, k * T:(k + 1) * T], u_first[k], mix_cols[:, kt:kt + 1],
                    m_hi[0][:, k * T:(k + 1) * T].bitcast(f32), ALU.mult, ALU.subtract).then_inc(m_lo_done, 1)
                if k == 0:
                    nc.vector.tensor_tensor(ssum, u_first[0], u_first[0], ALU.mult).then_inc(usq_added, 1)
                else:
                    dve.wait_ge(usq_done, k)
                    dve.wait_ge(usq_added, k)
                    ins = nc.vector.tensor_tensor(ssum, ssum, usq_first, ALU.add)
                    ins.then_inc(ssum_ready if k == GRP - 1 else usq_added, 1)

            decay_times_dt(HEADS - 1)
            for s in range(2 * TILES):
                step(s, HEADS - 1, None)
                if s == 0:
                    w2_split(0)
                if s == 1:
                    m_split_first(0)
                if s == 3:
                    for k in range(1, GRP):
                        m_split_first(k)
                if s == 5:
                    weights_in_chunks(HEADS - 1)
                if s == 9:
                    w2_split(1)
            dve.wait_ge(ua_stored, 16 * HEADS)
            dve.wait_ge(m_lo_done, GRP)
            dve.wait_ge(m_hi_done, GRP)

            def m_split(s, k):
                dve.wait_ge(m_hi_done, GRP * s + k + 1)
                kt = STEP_GROUPS[s] * GRP + k
                nc.vector.scalar_tensor_tensor(
                    m_lo[s % 2][:, k * T:(k + 1) * T], u_raw[:, k * T:(k + 1) * T], mix_cols[:, kt:kt + 1],
                    m_hi[s % 2][:, k * T:(k + 1) * T].bitcast(f32), ALU.mult, ALU.subtract).then_inc(m_lo_done, 1)
                if k == 0:
                    dve.wait_ge(stat_ready, s)
                    if s < 4:
                        nc.vector.tensor_tensor(ssum, u_raw[:, 0:T], u_raw[:, 0:T], ALU.mult).then_inc(usq_added, 1)
                    else:
                        copy(ssum, osq_sum[:, :]).then_inc(ssum_ready, 1)
                elif s < 4:
                    dve.wait_ge(usq_done, (GRP - 1) * s + k)
                    dve.wait_ge(usq_added, (GRP - 1) * s + k)
                    nc.vector.tensor_tensor(ssum, ssum, usq, ALU.add
                                            ).then_inc(ssum_ready if k == GRP - 1 else usq_added, 1)

            def finish(n):
                nb, t = LAST_ORDER[n]
                row = acc[:, t * D_MODEL:(t + 1) * D_MODEL]
                dve.wait_ge(fin_sq, n + 1)
                if nb == NB - 1:
                    did(nc.vector.tensor_reduce(fin_sum[:, t:t + 1], fin_parts[:, :, t], AX.X, ALU.add))
                    settle()
                    nc.vector.tensor_scalar(fin_mean[:, t:t + 1], fin_sum[:, t:t + 1], 1.0 / D_MODEL, EPS,
                                            ALU.mult, ALU.add).then_inc(fin_ms, 1)
                did(nc.vector.tensor_tensor(row[:, nb * NBW:(nb + 1) * NBW], row[:, nb * NBW:(nb + 1) * NBW],
                                            g_row[:, nb * NBW:(nb + 1) * NBW], ALU.mult))
                if nb == NB - 1:
                    dve.wait_ge(fin_root, t + 1)
                    did(nc.vector.reciprocal(fin_sum[:, t:t + 1], fin_rms[:, t:t + 1]))
                    settle()
                    dve.wait_ge(xb_in[t % XB], 16 * (t // XB + 1))
                    for h in range(2):
                        c0, c1 = h * D_MODEL // 2, (h + 1) * D_MODEL // 2
                        nc.vector.scalar_tensor_tensor(row[:, c0:c1], row[:, c0:c1], fin_sum[:, t:t + 1],
                                                       x_back[t % XB][:, c0:c1], ALU.mult, ALU.add
                                                       ).then_inc(fin_done, 1)

            def add_part(s, nb, t, n):
                dve.wait_ge(part_ready, TT * NB * s + n + 1)
                o = t * D_MODEL + nb * NBW
                r = r_cur[:, s % 2, t:t + 1]
                if s == 0:
                    nc.vector.tensor_scalar(acc[:, o:o + NBW], ps[:, n % TT, :], r, None, ALU.mult
                                            ).then_inc(acc_added, 1)
                    return
                dve.wait_ge(acc_added, TT * (NB * (s - 1) + nb) + t + 1)
                nc.vector.scalar_tensor_tensor(acc[:, o:o + NBW], ps[:, n % TT, :], r, acc[:, o:o + NBW],
                                               ALU.mult, ALU.add).then_inc(acc_added, 1)

            for s in range(STEPS):
                dve.wait_ge(stat_ready, s + 1)
                nc.vector.tensor_scalar(r_cur[:, s % 2, :], ps[:, 6, 0:TT],
                                        1.0 / (GRP * P if s < 4 else D_MODEL), EPS, ALU.mult, ALU.add
                                        ).then_inc(stat_read, 1)
                dve.wait_ge(r_root, s + 1)
                nc.vector.reciprocal(r_cur[:, s % 2, :], r_cur[:, s % 2, :]).then_inc(r_ready, 1)
                dve.wait_ge(r_ready, s + 1)
                if s == STEPS - 1:
                    break
                for nb in range(NB):
                    if s or nb:
                        w2_split(s * NB + nb + 1)
                    if s or nb >= 2:
                        m_split(s + 1, nb)
                    for t in range(TT):
                        add_part(s, nb, t, nb * TT + t)
                    if s == 0 and nb == 1:
                        m_split(1, 0)
                        m_split(1, 1)
            dve.wait_ge(g_in, 16)
            for n, (nb, t) in enumerate(LAST_ORDER):
                if nb == 0 and t < NB - 1:
                    w2_split(UNITS - NB + t + 1)
                add_part(STEPS - 1, nb, t, n)
                if n:
                    finish(n - 1)
            finish(len(LAST_ORDER) - 1)


_INS = ["x_prompt", "x_sample", "pre_norm_g", "w_in", "rel_bias_table", "attn_norm_g", "conv_w", "conv_b",
        "dt_bias_fwd", "dt_bias_bwd", "a_log_fwd", "a_log_bwd", "d_skip", "ssm_norm_g", "w_out", "post_norm_g"]
_SCRATCH = [("u_scr", (2 * 16 * 128, 768)), ("brow_scr", (16, 1024)), ("strip_scr", (16 * 128, 896)),
            ("loc_scr", (64, 768)), ("er_scr", (64, 768)), ("cb_scr", (4 * 128, PAIRS * 128 + 2 * 768))]


def kernel(**inputs):
    import concourse.bacc as bacc
    from concourse.bass_utils import run_bass_kernel_spmd

    nc = bacc.Bacc("TRN2", target_bir_lowering=False, num_devices=1, dynamic_dma_scratch_size=1024)
    f32 = mybir.dt.float32
    arrays, args = {}, []
    squares, hots = shape_constants()
    for name, a in [(n, inputs[n]) for n in _INS] + [("squares", squares), ("hots", hots)]:
        a = np.ascontiguousarray(a)
        arrays[f"in_{name}"] = a
        args.append(nc.dram_tensor(f"in_{name}", a.shape, f32, kind="ExternalInput").ap())
    for name, shape in _SCRATCH:
        args.append(nc.dram_tensor(name, shape, f32).ap())
    for name, shape in (("y_prompt", (1, SEQ, D_MODEL)), ("y_sample", (1, DEC_SEQ, D_MODEL))):
        args.append(nc.dram_tensor(name, shape, f32, kind="ExternalOutput").ap())
    encoder(nc, *args)
    r = run_bass_kernel_spmd(nc, [arrays], core_ids=[0])
    return r.results[0]["y_prompt"], r.results[0]["y_sample"]
```
